# Optimizing a Trainium2 kernel written in Bass

```python
import jax, jax.numpy as jnp
from jax import lax
import numpy as np
import math

D_MODEL = 1024
BATCH = 1
SEQ = 256
DEPTH = 2

HEAD_DIM = 64
N_SB_HEADS = 12
SB_WIDTH = N_SB_HEADS * HEAD_DIM
N_MEM_HEADS = 4
MEM_WIDTH = N_MEM_HEADS * HEAD_DIM
MEM_TOKENS = 256
MIX_WIDTH = SB_WIDTH + MEM_WIDTH
POOL_WINDOWS = (2, 4, 8, 16)
N_POOL_GROUPS = len(POOL_WINDOWS)
POOL_WIDTH = SB_WIDTH
POOL_GROUP = POOL_WIDTH // N_POOL_GROUPS
D_FF = -(-8 * D_MODEL // (3 * 256)) * 256
SB_BLOCK = 128
N_A_LAYERS = DEPTH // 2
N_B_LAYERS = DEPTH - N_A_LAYERS
EPS = 1e-6


def rmsnorm(x, g):
    xf = x.astype(jnp.float32)
    y = xf * lax.rsqrt(jnp.mean(xf * xf, axis=-1, keepdims=True) + EPS)
    return (y * g.astype(jnp.float32)).astype(x.dtype)

def swiglu(h, w_gu, w_down):
    gate, up = jnp.split(h @ w_gu, 2, axis=-1)
    return (jax.nn.silu(gate) * up) @ w_down

def multiscale_pool(u):
    s = u.shape[1]
    uf = u.astype(jnp.float32)
    cs = jnp.cumsum(uf, axis=1)
    pos = jnp.arange(s)
    outs = []
    for g, w in enumerate(POOL_WINDOWS):
        c = cs[..., g * POOL_GROUP:(g + 1) * POOL_GROUP]
        prev = jnp.pad(c, ((0, 0), (w, 0), (0, 0)))[:, :s]
        cnt = jnp.minimum(pos + 1, w).astype(jnp.float32)[None, :, None]
        outs.append((c - prev) / cnt)
    pooled = jnp.concatenate(outs, axis=-1)
    return (pooled - uf).astype(u.dtype)

def memory_kv(mem, mem_norm, w_mem_kv):
    b, m, _ = mem.shape
    k, v = jnp.split(rmsnorm(mem, mem_norm) @ w_mem_kv, 2, axis=-1)
    return (k.reshape(b, m, N_MEM_HEADS, HEAD_DIM), v.reshape(b, m, N_MEM_HEADS, HEAD_DIM))

def memory_attention(q, mk, mv):
    b, s, _ = q.shape
    qh = q.reshape(b, s, N_MEM_HEADS, HEAD_DIM)
    logits = jnp.einsum("bshd,bmhd->bhsm", qh, mk).astype(jnp.float32) * (HEAD_DIM ** -0.5)
    p = jax.nn.softmax(logits, axis=-1).astype(mv.dtype)
    return jnp.einsum("bhsm,bmhd->bshd", p, mv).reshape(b, s, MEM_WIDTH)

def stick_breaking_attention(q, k, v):
    s = q.shape[2]
    scale = HEAD_DIM ** -0.5
    outs = []
    for i in range(s // SB_BLOCK):
        q0 = i * SB_BLOCK
        end = q0 + SB_BLOCK
        qb = q[:, :, q0:end]
        kb = k[:, :, :end]
        vb = v[:, :, :end]
        z = jnp.einsum("bhqd,bhkd->bhqk", qb, kb).astype(jnp.float32) * scale
        tpos = q0 + jnp.arange(SB_BLOCK)
        spos = jnp.arange(end)
        mask = spos[None, :] < tpos[:, None]
        log_not = jnp.where(mask, jax.nn.log_sigmoid(-z), 0.0)
        later = lax.cumsum(log_not, axis=3, reverse=True) - log_not
        wts = jnp.where(mask, jnp.exp(jax.nn.log_sigmoid(z) + later), 0.0)
        outs.append(jnp.einsum("bhqk,bhkd->bhqd", wts.astype(vb.dtype), vb))
    return jnp.concatenate(outs, axis=2)

def pool_layer(x, mem, mem_norm, norm_mix, w_in, w_group, scale, w_mem_kv, w_out, norm_ffn, w_gu, w_down):
    b, s, _ = x.shape
    proj = rmsnorm(x, norm_mix) @ w_in
    u_pool, q_mem = proj[..., :POOL_WIDTH], proj[..., POOL_WIDTH:]
    pooled = multiscale_pool(u_pool).reshape(b, s, N_POOL_GROUPS, POOL_GROUP)
    grouped = jnp.einsum("bsgc,gcd->bsgd", pooled, w_group).reshape(b, s, POOL_WIDTH) * scale
    mk, mv = memory_kv(mem, mem_norm, w_mem_kv)
    mem_out = memory_attention(q_mem, mk, mv)
    x = x + jnp.concatenate([grouped, mem_out], axis=-1) @ w_out
    return x + swiglu(rmsnorm(x, norm_ffn), w_gu, w_down)

def sb_layer(x, mem, k_sh, v_sh, mem_norm, norm_mix, w_q, w_mem_kv, w_out, norm_ffn, w_gu, w_down):
    b, s, _ = x.shape
    proj = rmsnorm(x, norm_mix) @ w_q
    q_sb = proj[..., :SB_WIDTH].reshape(b, s, N_SB_HEADS, HEAD_DIM).transpose(0, 2, 1, 3)
    q_mem = proj[..., SB_WIDTH:]
    sb_out = stick_breaking_attention(q_sb, k_sh, v_sh).transpose(0, 2, 1, 3).reshape(b, s, SB_WIDTH)
    mk, mv = memory_kv(mem, mem_norm, w_mem_kv)
    mem_out = memory_attention(q_mem, mk, mv)
    x = x + jnp.concatenate([sb_out, mem_out], axis=-1) @ w_out
    return x + swiglu(rmsnorm(x, norm_ffn), w_gu, w_down)

def first_inputs(seed: int = 0) -> dict:
    key = jax.random.key(seed)
    ks = jax.random.split(key, 24)
    f32 = jnp.float32
    out_gain = (2.0 * DEPTH) ** -0.5

    def w(k, shape, fan_in, gain=1.0):
        return jax.random.normal(k, shape, f32) * (gain * fan_in ** -0.5)

    def g(k, shape):
        return 1.0 + 0.05 * jax.random.normal(k, shape, f32)

    na, nb = N_A_LAYERS, N_B_LAYERS
    return {
        "x": jax.random.normal(ks[0], (BATCH, SEQ, D_MODEL), f32),
        "mem": jax.random.normal(ks[1], (BATCH, MEM_TOKENS, D_MODEL), f32),
        "mem_norm": g(ks[2], (D_MODEL,)),
        "a_norm_mix": g(ks[3], (na, D_MODEL)),
        "a_w_in": w(ks[4], (na, D_MODEL, MIX_WIDTH), D_MODEL),
        "a_w_group": w(ks[5], (na, N_POOL_GROUPS, POOL_GROUP, POOL_GROUP), POOL_GROUP),
        "a_scale": g(ks[6], (na, POOL_WIDTH)),
        "a_w_mem_kv": w(ks[7], (na, D_MODEL, 2 * MEM_WIDTH), D_MODEL),
        "a_w_out": w(ks[8], (na, MIX_WIDTH, D_MODEL), MIX_WIDTH, out_gain),
        "a_norm_ffn": g(ks[9], (na, D_MODEL)),
        "a_w_gu": w(ks[10], (na, D_MODEL, 2 * D_FF), D_MODEL),
        "a_w_down": w(ks[11], (na, D_FF, D_MODEL), D_FF, out_gain),
        "kv_norm": g(ks[12], (D_MODEL,)),
        "w_kv": w(ks[13], (D_MODEL, 2 * SB_WIDTH), D_MODEL),
        "b_norm_mix": g(ks[14], (nb, D_MODEL)),
        "b_w_q": w(ks[15], (nb, D_MODEL, MIX_WIDTH), D_MODEL),
        "b_w_mem_kv": w(ks[16], (nb, D_MODEL, 2 * MEM_WIDTH), D_MODEL),
        "b_w_out": w(ks[17], (nb, MIX_WIDTH, D_MODEL), MIX_WIDTH, out_gain),
        "b_norm_ffn": g(ks[18], (nb, D_MODEL)),
        "b_w_gu": w(ks[19], (nb, D_MODEL, 2 * D_FF), D_MODEL),
        "b_w_down": w(ks[20], (nb, D_FF, D_MODEL), D_FF, out_gain),
        "final_norm": g(ks[21], (D_MODEL,)),
    }

def first_block(x, mem, mem_norm, a_norm_mix, a_w_in, a_w_group, a_scale, a_w_mem_kv, a_w_out,
              a_norm_ffn, a_w_gu, a_w_down, kv_norm, w_kv, b_norm_mix, b_w_q, b_w_mem_kv,
              b_w_out, b_norm_ffn, b_w_gu, b_w_down, final_norm):
    b, s, _ = x.shape
    k_sh = v_sh = None
    for layer in range(DEPTH):
        if layer < N_A_LAYERS:
            i = layer
            x = pool_layer(x, mem, mem_norm, a_norm_mix[i], a_w_in[i], a_w_group[i], a_scale[i],
                           a_w_mem_kv[i], a_w_out[i], a_norm_ffn[i], a_w_gu[i], a_w_down[i])
        else:
            if layer == N_A_LAYERS:
                kv = rmsnorm(x, kv_norm) @ w_kv
                k_sh = kv[..., :SB_WIDTH].reshape(b, s, N_SB_HEADS, HEAD_DIM).transpose(0, 2, 1, 3)
                v_sh = kv[..., SB_WIDTH:].reshape(b, s, N_SB_HEADS, HEAD_DIM).transpose(0, 2, 1, 3)
            j = layer - N_A_LAYERS
            x = sb_layer(x, mem, k_sh, v_sh, mem_norm, b_norm_mix[j], b_w_q[j], b_w_mem_kv[j],
                         b_w_out[j], b_norm_ffn[j], b_w_gu[j], b_w_down[j])
    return rmsnorm(x, final_norm)


DEPTH_2 = 1

N_HEADS_A = 8
N_IDX_HEADS = 8
IDX_DIM = 32
TOPK_TOKENS = 256
N_HEADS_B = 8
N_KV_GROUPS_B = 2
HEADS_PER_GROUP = N_HEADS_B // N_KV_GROUPS_B
CMP_BLOCK = 32
CMP_STRIDE = 16
CMP_HIDDEN = 128
SLC_BLOCK = 64
N_SLC_BLOCKS = 16
WINDOW = 512
FORCED_SCORE = 1.0e4
N_BUCKETS = 32
MAX_DISTANCE = 128
D_FF_2 = 4 * D_MODEL
Q_BLOCK_A = 128
Q_BLOCK_B = 64

W_QA = N_HEADS_A * HEAD_DIM
W_KA = HEAD_DIM
W_VA = HEAD_DIM
W_QI = N_IDX_HEADS * IDX_DIM
W_KI = IDX_DIM
W_WI = N_IDX_HEADS
W_QB = N_HEADS_B * HEAD_DIM
W_KVB = 6 * N_KV_GROUPS_B * HEAD_DIM
W_GB = 3 * N_HEADS_B
W_GATE = 2 * D_MODEL
D_IN = W_QA + W_KA + W_VA + W_QI + W_KI + W_WI + W_QB + W_KVB + W_GB + W_GATE


def rmsnorm_2(x, g):
    xf = x.astype(jnp.float32)
    y = xf * lax.rsqrt(jnp.mean(xf * xf, axis=-1, keepdims=True) + EPS)
    return (y * g.astype(jnp.float32)).astype(x.dtype)

def t5_bucket(dist):
    n = jnp.maximum(dist, 0)
    max_exact = N_BUCKETS // 2
    nf = jnp.maximum(n, 1).astype(jnp.float32)
    large = max_exact + (jnp.log(nf / max_exact) / math.log(MAX_DISTANCE / max_exact)
                         * (N_BUCKETS - max_exact)).astype(jnp.int32)
    large = jnp.minimum(large, N_BUCKETS - 1)
    return jnp.where(n < max_exact, n, large)

def masked_softmax(logits, mask):
    lf = jnp.where(mask, logits.astype(jnp.float32), -jnp.inf)
    m = jnp.max(lf, axis=-1, keepdims=True)
    m = jnp.where(jnp.isfinite(m), m, 0.0)
    e = jnp.where(mask, jnp.exp(lf - m), 0.0)
    return e / jnp.maximum(jnp.sum(e, axis=-1, keepdims=True), 1e-30)

def dsa_mixer(q_a, k_a, v_a, q_i, k_i, w_i, table_a):
    B, S = q_a.shape[:2]
    k_top = min(TOPK_TOKENS, S // 4)
    n_blk = S // Q_BLOCK_A
    scale = HEAD_DIM ** -0.5
    w_scale = (N_IDX_HEADS ** -0.5) * (IDX_DIM ** -0.5)
    key_pos = jnp.arange(S)
    gather = jax.vmap(lambda kb, ib: kb[ib])

    def block(i):
        q0 = i * Q_BLOCK_A
        t = q0 + jnp.arange(Q_BLOCK_A)
        qi = lax.dynamic_slice_in_dim(q_i, q0, Q_BLOCK_A, axis=1)
        wi = lax.dynamic_slice_in_dim(w_i, q0, Q_BLOCK_A, axis=1).astype(jnp.float32) * w_scale
        s_h = jnp.einsum('bqhd,bsd->bqhs', qi, k_i).astype(jnp.float32)
        score = jnp.einsum('bqh,bqhs->bqs', wi, jax.nn.relu(s_h))
        causal = key_pos[None, :] <= t[:, None]
        score = jnp.where(causal[None], score, -jnp.inf)
        _, idx = lax.top_k(score, k_top)
        k_sel = gather(k_a, idx)
        v_sel = gather(v_a, idx)
        qa = lax.dynamic_slice_in_dim(q_a, q0, Q_BLOCK_A, axis=1)
        dist = t[None, :, None] - idx
        bias = table_a[t5_bucket(dist)].transpose(0, 1, 3, 2)
        logits = jnp.einsum('bqhd,bqkd->bqhk', qa, k_sel) * scale + bias
        p = masked_softmax(logits, (dist >= 0)[:, :, None, :])
        o = jnp.einsum('bqhk,bqkd->bqhd', p.astype(v_sel.dtype), v_sel)
        return o.reshape(B, Q_BLOCK_A, N_HEADS_A * HEAD_DIM)

    out = lax.map(block, jnp.arange(n_blk))
    return out.transpose(1, 0, 2, 3).reshape(B, S, N_HEADS_A * HEAD_DIM)

def compress_blocks(kv, pe, w1, w2):
    B, S, G, D = kv.shape
    n_c = (S - CMP_BLOCK) // CMP_STRIDE + 1
    idx = jnp.arange(n_c)[:, None] * CMP_STRIDE + jnp.arange(CMP_BLOCK)[None, :]
    blk = kv[:, idx] + pe[None, None, :, None, :]
    blk = blk.transpose(0, 1, 3, 2, 4).reshape(B, n_c, G, CMP_BLOCK * D)
    return jax.nn.gelu(blk @ w1) @ w2

def nsa_mixer(q, kc, vc, ks, vs, kw, vw, gates, pe_k, w1_k, w2_k, pe_v, w1_v, w2_v, table_b):
    B, S = q.shape[:2]
    G, R, D = N_KV_GROUPS_B, HEADS_PER_GROUP, HEAD_DIM
    QB = Q_BLOCK_B
    scale = D ** -0.5
    q = q.reshape(B, S, G, R, D)
    gates = jax.nn.sigmoid(gates.astype(jnp.float32)).reshape(B, S, 3, G, R)
    kc_cmp = compress_blocks(kc, pe_k, w1_k, w2_k)
    vc_cmp = compress_blocks(vc, pe_v, w1_v, w2_v)
    n_c = kc_cmp.shape[1]
    n_s = S // SLC_BLOCK
    n_sel = min(N_SLC_BLOCKS, n_s)
    cmp_start = jnp.arange(n_c) * CMP_STRIDE
    cmp_end = cmp_start + CMP_BLOCK - 1
    slc_start = jnp.arange(n_s) * SLC_BLOCK
    overlap = jnp.clip(jnp.minimum(cmp_start[:, None] + CMP_BLOCK, slc_start[None, :] + SLC_BLOCK)
                       - jnp.maximum(cmp_start[:, None], slc_start[None, :]), 0, None
                       ).astype(jnp.float32) / CMP_BLOCK
    ks_blk = ks.reshape(B, n_s, SLC_BLOCK, G, D).transpose(0, 3, 1, 2, 4)
    vs_blk = vs.reshape(B, n_s, SLC_BLOCK, G, D).transpose(0, 3, 1, 2, 4)
    gather = jax.vmap(jax.vmap(lambda kb, ib: kb[ib]))
    pad = ((0, 0), (WINDOW, 0), (0, 0), (0, 0))
    kw_p = jnp.pad(kw, pad)
    vw_p = jnp.pad(vw, pad)
    tg = table_b.reshape(N_BUCKETS, G, R).transpose(1, 0, 2)
    g_idx = jnp.arange(G)[None, :, None, None]
    blk_id = jnp.arange(n_s)
    KW = WINDOW + QB

    def block(i):
        q0 = i * QB
        t = q0 + jnp.arange(QB)
        qb = lax.dynamic_slice_in_dim(q, q0, QB, axis=1)
        gb = lax.dynamic_slice_in_dim(gates, q0, QB, axis=1)
        dist_c = t[:, None] - cmp_end[None, :]
        bias_c = table_b[t5_bucket(dist_c)].reshape(QB, n_c, G, R).transpose(0, 2, 3, 1)
        logit_c = jnp.einsum('bqgrd,bcgd->bqgrc', qb, kc_cmp) * scale + bias_c
        p_c = masked_softmax(logit_c, (dist_c >= 0)[:, None, None, :])
        o_c = jnp.einsum('bqgrc,bcgd->bqgrd', p_c.astype(vc_cmp.dtype), vc_cmp)
        imp = jnp.einsum('bqgrc,cn->bqgn', p_c, overlap)
        cur = t // SLC_BLOCK
        valid = blk_id[None, :] <= cur[:, None]
        forced = ((blk_id[None, :] == 0) | (blk_id[None, :] == cur[:, None])
                  | (blk_id[None, :] == cur[:, None] - 1))
        score = jnp.where(valid[None, :, None, :],
                          jnp.where(forced[None, :, None, :], FORCED_SCORE, imp), -jnp.inf)
        _, sel = lax.top_k(score, n_sel)
        sel_t = sel.transpose(0, 2, 1, 3)
        k_sel = gather(ks_blk, sel_t).reshape(B, G, QB, n_sel * SLC_BLOCK, D)
        v_sel = gather(vs_blk, sel_t).reshape(B, G, QB, n_sel * SLC_BLOCK, D)
        pos_s = (sel_t[..., None] * SLC_BLOCK + jnp.arange(SLC_BLOCK)).reshape(B, G, QB, n_sel * SLC_BLOCK)
        dist_s = t[None, None, :, None] - pos_s
        bias_s = tg[g_idx, t5_bucket(dist_s)].transpose(0, 1, 2, 4, 3)
        logit_s = jnp.einsum('bqgrd,bgqkd->bgqrk', qb, k_sel) * scale + bias_s
        p_s = masked_softmax(logit_s, (dist_s >= 0)[:, :, :, None, :])
        o_s = jnp.einsum('bgqrk,bgqkd->bqgrd', p_s.astype(v_sel.dtype), v_sel)
        kwb = lax.dynamic_slice_in_dim(kw_p, q0, KW, axis=1)
        vwb = lax.dynamic_slice_in_dim(vw_p, q0, KW, axis=1)
        pos_w = q0 - WINDOW + jnp.arange(KW)
        dist_w = t[:, None] - pos_w[None, :]
        mask_w = (dist_w >= 0) & (dist_w < WINDOW) & (pos_w[None, :] >= 0)
        bias_w = table_b[t5_bucket(dist_w)].reshape(QB, KW, G, R).transpose(0, 2, 3, 1)
        logit_w = jnp.einsum('bqgrd,bkgd->bqgrk', qb, kwb) * scale + bias_w
        p_w = masked_softmax(logit_w, mask_w[:, None, None, :])
        o_w = jnp.einsum('bqgrk,bkgd->bqgrd', p_w.astype(vwb.dtype), vwb)
        o = (gb[:, :, 0, :, :, None] * o_c + gb[:, :, 1, :, :, None] * o_s
             + gb[:, :, 2, :, :, None] * o_w)
        return o.astype(q.dtype).reshape(B, QB, G * R * D)

    out = lax.map(block, jnp.arange(S // QB))
    return out.transpose(1, 0, 2, 3).reshape(B, S, N_HEADS_B * HEAD_DIM)

def second_inputs(seed: int = 0) -> dict:
    key = jax.random.key(seed)
    ks = jax.random.split(key, 20)
    f32 = jnp.float32
    nrm = lambda k, shape, s: jax.random.normal(k, shape, f32) * s
    L, D = CMP_BLOCK, HEAD_DIM
    return {
        "x": nrm(ks[0], (BATCH, SEQ, D_MODEL), 1.0),
        "norm_mix": 1.0 + nrm(ks[1], (DEPTH_2, D_MODEL), 0.02),
        "w_in": nrm(ks[2], (DEPTH_2, D_MODEL, D_IN), D_MODEL ** -0.5),
        "cmp_pe_k": nrm(ks[3], (DEPTH_2, L, D), 0.1),
        "cmp_w1_k": nrm(ks[4], (DEPTH_2, L * D, CMP_HIDDEN), (L * D) ** -0.5),
        "cmp_w2_k": nrm(ks[5], (DEPTH_2, CMP_HIDDEN, D), CMP_HIDDEN ** -0.5),
        "cmp_pe_v": nrm(ks[6], (DEPTH_2, L, D), 0.1),
        "cmp_w1_v": nrm(ks[7], (DEPTH_2, L * D, CMP_HIDDEN), (L * D) ** -0.5),
        "cmp_w2_v": nrm(ks[8], (DEPTH_2, CMP_HIDDEN, D), CMP_HIDDEN ** -0.5),
        "rel_bias": nrm(ks[9], (N_BUCKETS, N_HEADS_A + N_HEADS_B), 0.5),
        "w_branch_a": nrm(ks[10], (DEPTH_2, W_QA, D_MODEL), W_QA ** -0.5),
        "w_branch_b": nrm(ks[11], (DEPTH_2, W_QB, D_MODEL), W_QB ** -0.5),
        "w_out": nrm(ks[12], (DEPTH_2, D_MODEL, D_MODEL), D_MODEL ** -0.5),
        "norm_mlp": 1.0 + nrm(ks[13], (DEPTH_2, D_MODEL), 0.02),
        "w_mlp_in": nrm(ks[14], (DEPTH_2, D_MODEL, D_FF_2), D_MODEL ** -0.5),
        "w_mlp_out": nrm(ks[15], (DEPTH_2, D_FF_2, D_MODEL), D_FF_2 ** -0.5),
        "norm_final": 1.0 + nrm(ks[16], (D_MODEL,), 0.02),
    }

def second_block(x, norm_mix, w_in, cmp_pe_k, cmp_w1_k, cmp_w2_k, cmp_pe_v, cmp_w1_v, cmp_w2_v,
              rel_bias, w_branch_a, w_branch_b, w_out, norm_mlp, w_mlp_in, w_mlp_out, norm_final):
    B, S, _ = x.shape
    G, D = N_KV_GROUPS_B, HEAD_DIM
    widths = [W_QA, W_KA, W_VA, W_QI, W_KI, W_WI, W_QB, W_KVB, W_GB, W_GATE]
    split_pts = [int(v) for v in np.cumsum(widths)[:-1]]
    table_a = rel_bias[:, :N_HEADS_A]
    table_b = rel_bias[:, N_HEADS_A:]
    for l in range(DEPTH_2):
        h = rmsnorm_2(x, norm_mix[l])
        proj = h @ w_in[l]
        q_a, k_a, v_a, q_i, k_i, w_i, q_b, kv_b, g_b, g_br = jnp.split(proj, split_pts, axis=-1)
        o_a = dsa_mixer(q_a.reshape(B, S, N_HEADS_A, D), k_a, v_a,
                        q_i.reshape(B, S, N_IDX_HEADS, IDX_DIM), k_i, w_i, table_a)
        kv_b = kv_b.reshape(B, S, 6, G, D)
        o_b = nsa_mixer(q_b.reshape(B, S, N_HEADS_B, D), kv_b[:, :, 0], kv_b[:, :, 1],
                        kv_b[:, :, 2], kv_b[:, :, 3], kv_b[:, :, 4], kv_b[:, :, 5], g_b,
                        cmp_pe_k[l], cmp_w1_k[l], cmp_w2_k[l], cmp_pe_v[l], cmp_w1_v[l],
                        cmp_w2_v[l], table_b)
        gate_a, gate_b = jnp.split(g_br, 2, axis=-1)
        mix = (jax.nn.sigmoid(gate_a) * (o_a @ w_branch_a[l])
               + jax.nn.sigmoid(gate_b) * (o_b @ w_branch_b[l]))
        x = x + mix @ w_out[l]
        h = rmsnorm_2(x, norm_mlp[l])
        x = x + jnp.square(jax.nn.relu(h @ w_mlp_in[l])) @ w_mlp_out[l]
    return rmsnorm_2(x, norm_final)


def setup_inputs(seed=0):
    out = dict(first_inputs(seed))
    for name, value in second_inputs(seed + 1).items():
        if name != "x":
            out[name + "_2"] = value
    return out


def reference(
    x, mem, mem_norm, a_norm_mix, a_w_in, a_w_group, a_scale, a_w_mem_kv, a_w_out, a_norm_ffn,
    a_w_gu, a_w_down, kv_norm, w_kv, b_norm_mix, b_w_q, b_w_mem_kv, b_w_out, b_norm_ffn, b_w_gu,
    b_w_down, final_norm, norm_mix_2, w_in_2, cmp_pe_k_2, cmp_w1_k_2, cmp_w2_k_2, cmp_pe_v_2,
    cmp_w1_v_2, cmp_w2_v_2, rel_bias_2, w_branch_a_2, w_branch_b_2, w_out_2, norm_mlp_2,
    w_mlp_in_2, w_mlp_out_2, norm_final_2,
):
    x = first_block(
        x, mem, mem_norm, a_norm_mix, a_w_in, a_w_group, a_scale, a_w_mem_kv, a_w_out,
        a_norm_ffn, a_w_gu, a_w_down, kv_norm, w_kv, b_norm_mix, b_w_q, b_w_mem_kv, b_w_out,
        b_norm_ffn, b_w_gu, b_w_down, final_norm,
    )
    return second_block(
        x, norm_mix_2, w_in_2, cmp_pe_k_2, cmp_w1_k_2, cmp_w2_k_2, cmp_pe_v_2, cmp_w1_v_2,
        cmp_w2_v_2, rel_bias_2, w_branch_a_2, w_branch_b_2, w_out_2, norm_mlp_2, w_mlp_in_2,
        w_mlp_out_2, norm_final_2,
    )


_drawn_inputs = setup_inputs


def setup_inputs(seed=0):
    import zlib

    import numpy as np

    out = dict(_drawn_inputs(seed))
    spreads = {}
    factors = {'mem_norm': 8.0,
     'kv_norm': 2.841,
     'b_norm_mix': 4.897,
     'norm_mix_2': 3.283,
     'cmp_pe_k_2': 8.0,
     'cmp_pe_v_2': 3.078,
     'norm_mlp_2': 3.141,
     'norm_final_2': 2.727}
    for name, (base, spread) in spreads.items():
        noise = np.random.default_rng([zlib.crc32(name.encode()), seed]).standard_normal(out[name].shape)
        drawn = base * np.exp(spread * noise) if base else spread * noise
        out[name] = __import__('jax').numpy.asarray(drawn.astype(out[name].dtype))
    for name, factor in factors.items():
        out[name] = (out[name] * factor).astype(out[name].dtype)
    return out
```

```python
from contextlib import ExitStack

import numpy as np
import concourse.bass as bass
from concourse import mybir

S = 256
D = 1024
P = 128
KC = D // P
FF1 = 2816
FF2 = 4096
SB = 768
HD = 64
UNIT = 2048
NRAW = 4
W_FRONT = 2240
EPS = 1e-6
NEG = -1.0e30
TAKEN = -3.0e38
TABLE_J0 = 255
C_QA, C_KA, C_VA, C_QI, C_KI, C_WI, C_QB, C_KVB, C_GB = 0, 512, 576, 640, 896, 928, 936, 1448, 2216
C_KC, C_VC, C_KS, C_VS, C_KW, C_VW = (C_KVB + 128 * n for n in range(6))

JOBS = [("mem_a", 2, 1, "act"), ("mem_b", 2, 1, "act"), ("in", 4, 2, "act"), ("a_out", 4, 2, "dve"),
        ("a_gu", 22, 11, "dve"), ("a_down", 11, 2, "dve"), ("kv", 6, 3, "act"), ("q", 4, 2, "act"),
        ("b_out", 4, 2, "dve"), ("b_gu", 22, 11, "dve"), ("b_down", 11, 2, "dve"), ("front", 8, 4, "act"),
        ("front_rest", 1, 1, "act"), ("cmp", 2, 0, ""), ("gates", 8, 4, "act"), ("branch_a", 2, 2, "dve"),
        ("branch_b", 2, 2, "dve"), ("out2", 4, 2, "dve"), ("up2", 16, 8, "act"), ("down2", 16, 2, "dve")]
U0, G0, EMPTIED_BY = {}, {}, []
_u = 0
for _n, _c, _g, _e in JOBS:
    U0[_n], G0[_n] = _u, len(EMPTIED_BY)
    _u += _c
    EMPTIED_BY += [_e] * _g


def emptied(g, engine):
    return EMPTIED_BY[:g + 1].count(engine)


GAMMAS = ["mem_norm", "a_norm_mix", "a_norm_ffn", "kv_norm", "b_norm_mix", "b_norm_ffn", "norm_mix_2",
          "norm_mlp_2"]
NGROW = 8 * len(GAMMAS) + SB // P
NORM = {n: i for i, n in enumerate(["mem", "a_mix", "a_ffn", "b_mix", "b_ffn", "final1", "mix2", "mlp2", "final2"])}
A0 = {"mem_a": 0, "mem_b": 4, "nsa": 8, "dsa": 24}
O0 = {"mem_a": 0, "sb": 2, "mem_b": 8, "nsa": 10, "dsa": 14}


def build(nc, A):
    fp32, f32r = mybir.dt.float32, mybir.dt.float32r
    ACT, ALU, AX = mybir.ActivationFunctionType, mybir.AluOpType, mybir.AxisListType
    ctx = ExitStack()
    with ctx:
        def sem(name):
            return ctx.enter_context(nc.semaphore(name))

        first = (nc.sbuf_base + 31) // 32 * 32
        plan = {"at": 0}

        def place(name, cols, dt=fp32, at=None):
            if at is None:
                at = plan["at"]
                plan["at"] += cols
            return nc.alloc_sbuf_tensor_at(name, [P, cols], dt, offset=first + 4 * at)

        raw = place("raw", NRAW * UNIT)
        w_hi = place("w_hi", 2 * UNIT, f32r)
        w_lo = place("w_lo", 2 * UNIT, f32r)
        x_sb = place("x_sb", 2 * D)
        a_hi = place("a_hi", KC * S, f32r)
        a_lo = place("a_lo", KC * S, f32r)
        m_hi = place("m_hi", KC * S, f32r)
        m_lo = place("m_lo", KC * S, f32r)
        ident = place("ident", P)
        gam = place("gam", NGROW + 2)
        tiny = place("tiny", 256)
        r1 = plan["at"]
        h_hi = place("h_hi", 32 * S, f32r)
        h_lo = place("h_lo", 32 * S, f32r)
        r2 = plan["at"]
        xn = place("xn", 2 * D)
        kvm = place("kvm", 2 * 2 * 512)
        work_b = plan["at"]
        pb = place("pb", 2 * 512)
        pt = place("pt", 2 * 512)
        sc = place("sc", 512)
        sel = place("sel", 512)
        sbc = place("sbc", 2 * P + 768, at=plan["at"] - 1024)
        caus = place("caus", 512)
        pc = place("pc", 512)
        pct = place("pct", 512)
        cw = place("cw", 706)
        gates = place("gates", 2 * 2 * D, at=r2)
        mlp_a = place("mlp_a", 2 * 1024, at=r2)
        mlp_b = place("mlp_b", 2 * 1024, at=work_b)
        gfin = place("gfin", D, at=work_b)
        assert first + 4 * plan["at"] <= nc.sbuf_usable_end, (first + 4 * plan["at"], nc.sbuf_usable_end)

        cur = {"at": r1}

        def over(name, cols):
            t = place(name, cols, at=cur["at"])
            cur["at"] += cols
            assert cur["at"] <= r2, name
            return t

        projA = over("projA", 2 * D)
        memx = over("memx", 2 * D)
        qTA = over("qTA", 512)
        mkTA = over("mkTA", 512)
        poolT = over("poolT", 8 * S)
        poolM = over("poolM", 2 * 4 * S)
        wgrp = over("wgrp", 8 * 192)
        stage = over("stage", 512 + 16)
        gamrow = over("gamrow", P)
        relb = over("relb", 16)
        onehot = over("onehot", 512)
        cur["at"] = r1
        kvB = over("kvB", 2 * 2 * SB)
        qB = over("qB", 2 * D)
        qTB = over("qTB", 8 * S)
        kTB = over("kTB", 6 * S)
        mkTB = over("mkTB", 512)
        sbE = over("sbE", 2 * 384)
        sbL = over("sbL", 2 * 384)
        sbW = over("sbW", 2 * 384)
        cur["at"] = r1
        strip = over("strip", 16 * 384)
        front = over("front", 2 * W_FRONT)
        TT = over("TT", 16 * S)

        ps = ctx.enter_context(nc.psum_tensor("ps", [P, 8, 512], fp32))
        L0, TB, OB = 4, 6, 2

        s_raw = [sem(f"raw_loaded{i}") for i in range(NRAW)]
        s_hi, s_lo, s_mm = sem("hi_split"), sem("lo_split"), sem("unit_multiplied")
        s_gact, s_gdve = sem("groups_emptied_act"), sem("groups_emptied_dve")
        s_x, s_mem, s_cst, s_gin, s_pin, s_out = (sem(n) for n in ("x_loaded", "mem_loaded", "consts_loaded",
                                                                  "rows_loaded", "pool_loaded", "out_stored"))
        s_tabp, s_tab, s_tabd, s_strip = sem("table_product"), sem("table_copied"), sem("table_stored"), sem("strips_loaded")
        s_gamT, s_gam = sem("gamma_transposed"), sem("gamma_copied")
        s_ssq, s_var, s_std, s_xn = sem("squares_summed"), sem("variance"), sem("std"), sem("normed")
        s_tp, s_nhi, s_nlo = sem("normed_transposed"), sem("normed_hi"), sem("normed_lo")
        s_dve, s_act = sem("dve_chain"), sem("act_chain")
        s_gfin = sem("final_gamma_loaded")
        s_pool, s_poolc, s_grp = sem("pooled"), sem("pooled_copied"), sem("grouped")
        s_ghi, s_glo = sem("grouped_hi"), sem("grouped_lo")
        s_qk, s_qkc = sem("qk_transposed"), sem("qk_copied")
        s_lg, s_m, s_e, s_p = sem("logits"), sem("row_max"), sem("exps"), sem("probs")
        s_pt, s_ptc, s_pv = sem("probs_transposed"), sem("probsT_copied"), sem("values_mixed")
        s_ohi, s_olo = sem("pair_hi"), sem("pair_lo")
        s_z, s_sbe, s_sbl, s_tri, s_arg, s_wt, s_sbpv = (sem(n) for n in ("sb_scores", "sb_log1p", "sb_softplus",
            "sb_summed", "sb_exponent", "sb_weights", "sb_mixed"))
        s_sg, s_hb, s_ht, s_hhi, s_hlo = (sem(n) for n in ("gate_act", "hidden", "hidden_transposed",
                                                         "hidden_hi", "hidden_lo"))
        s_x2p, s_x2h, s_x2, s_hid, s_gel, s_cmpp, s_cmpc = (sem(n) for n in ("cmp_tokens", "cmp_hi", "cmp_lo",
            "cmp_hidden", "cmp_gelu", "cmp_kv", "cmp_kv_copied"))
        s_uarg, s_tanh = sem("gelu_arg"), sem("gelu_tanh")
        s_clg, s_clm, s_cex, s_cp, s_cpt, s_cptc = (sem(n) for n in ("cmp_logits", "cmp_shifted", "cmp_exps",
            "cmp_probs", "cmp_probsT", "cmp_probsT_copied"))
        s_gb, s_ix, s_rl, s_ac, s_top = (sem(n) for n in ("head_gates", "index_products", "index_relu",
                                                       "index_summed", "top_selected"))
        s_mx = sem("branches_mixed")
        s_fin = sem("final_rows")
        s_ind = sem("cmp_inputs_loaded")

        s_gm = sem("gated_product")
        s_peT, s_pec, s_x2t = sem("embeddings_transposed"), sem("embeddings_copied"), sem("cmp_tokens_transposed")

        def tok(t, cols, T):
            return t[:, T * cols:(T + 1) * cols]

        def ch(t, c, n=1):
            return t[:, c * S:(c + n) * S]

        def chT(t, c, T):
            return t[:, c * S + T * P:c * S + (T + 1) * P]

        def bank(b, lo=0, hi=512):
            return ps[:, b, lo:hi]

        def pair_banks(q, lo=0, hi=512):
            return ps[:, 2 * q:2 * q + 2, lo:hi]

        def ring(t, slots, u):
            return t[:, (u % slots) * UNIT:(u % slots + 1) * UNIT]

        sb_tri, sb_ones = sbc[:, 0:P], sbc[:, P:2 * P]
        sb_mask, sb_neg = sbc[:, 256:640], sbc[:, 640:1024]

        ssq, var, std, rst, t1, t2 = (tiny[:, 2 * n:2 * n + 2] for n in range(6))
        nmax = [tiny[:, 16 + 2 * n:18 + 2 * n] for n in range(2)]
        rsum = [tiny[:, 20 + 2 * n:22 + 2 * n] for n in range(2)]
        rrec = [tiny[:, 24 + 2 * n:26 + 2 * n] for n in range(2)]
        cmx, csum, crec = (tiny[:, 32 + 16 * n:48 + 16 * n] for n in range(3))
        gb = tiny[:, 80:128]
        wi = tiny[:, 128:144]
        top8 = tiny[:, 144:160]
        gel = cw[:, 0:60]
        ga1, ga2, gth = cw[:, 80:140], cw[:, 140:200], cw[:, 200:260]
        kcmpT = cw[:, 260:290]
        vcmp = cw[:, 290:418]
        peT = cw[:, 418:450]
        w2 = cw[:, 450:578]
        per = cw[0:32, 578:706]
        x2h, x2l = m_hi[:, 0:960], m_lo[:, 0:960]
        pc_v = pc[:, :].rearrange("p (h n) -> p h n", h=16)[:, :, 0:15]

        block = ctx.enter_context(nc.Block())
        PASSES = ((0, 0), (0, 1), (1, 0))

        @block.sync
        def _(sp):
            sp.dma_start(x_sb[:, :].rearrange("p (t d) -> p t d", t=2),
                         A["x"].rearrange("(t p) d -> p t d", p=P)).then_inc(s_x, 16)
            sp.dma_start(memx[:, :].rearrange("p (t d) -> p t d", t=2),
                         A["mem"].rearrange("(t p) d -> p t d", p=P)).then_inc(s_mem, 16)

            def load(us, i, src, n=UNIT):
                if not (isinstance(i, int) and us + 4 * i < NRAW):
                    sp.wait_ge(s_lo, 4 * i + us - NRAW + 1)
                sp.dma_start(ring(raw, NRAW, us)[:, 0:n], src).then_inc(s_raw[us % NRAW], 16)

            def job(name, lo=0, hi=None):
                for j in range(lo, hi or dict((n, c) for n, c, _, _ in JOBS)[name]):
                    load(U0[name] + j, 0, A[name][j * P:(j + 1) * P, :])

            def job_loop(name, lo, n):
                with sp.Fori(0, n) as i:
                    for j in range(lo, lo + 4):
                        load(U0[name] + j, i, A[name][bass.ds(P * j + 4 * P * i, P), :])

            for name in ("mem_a", "mem_b", "in", "a_out"):
                job(name)
            job("a_gu", 0, 2)
            job_loop("a_gu", 2, 5)
            for name in ("a_down", "kv", "q", "b_out"):
                job(name)
            job("b_gu", 0, 2)
            job_loop("b_gu", 2, 5)
            for name in ("b_down", "front"):
                job(name)
            load(U0["front_rest"], 0, A["front_rest"], 8 * 192)
            for name in ("cmp", "gates", "branch_a", "branch_b", "out2"):
                job(name)
            job_loop("up2", 0, 4)
            job_loop("down2", 0, 4)
            for T in range(2):
                sp.wait_ge(s_fin, T + 2)
                sp.dma_start(A["out"][T * P:(T + 1) * P, :], tok(xn, D, T)).then_inc(s_out, 16)
            sp.wait_ge(s_out, 32)

        @block.gpsimd
        def _(pool):
            pool.wait_ge(s_tab, 1)
            pool.dma_start(A["table"], stage[0:16, 0:512]).then_inc(s_tabd, 16)
            pool.wait_ge(s_mm, U0["b_down"] + 1)
            pool.dma_start(gfin[:, :], A["final_norm"].partition_broadcast(P)).then_inc(s_gfin, 16)
            pool.wait_ge(s_mm, U0["b_down"] + 11)
            pool.wait_ge(s_tabd, 16)
            pool.dma_start(strip[:, :].rearrange("p (h c) -> p h c", h=16),
                           bass.AP(A["table"].tensor, 0, [[1, P], [512, 16], [1, 384]])).then_inc(s_strip, 16)
            pool.dma_start(caus[:, :], A["causal"]).then_inc(s_strip, 16)
            for n, kv in enumerate(("k", "v")):
                pool.dma_start(per[16 * n:16 * n + 16, :], A[f"cmp_pe_{kv}_2"].rearrange("(j r) d -> j (r d)", r=2))\
                    .then_inc(s_ind, 16)
                pool.dma_start(w2[:, HD * n:HD * n + HD], A[f"cmp_w2_{kv}_2"]).then_inc(s_ind, 16)
            pool.wait_ge(s_mm, U0["down2"] + 1)
            pool.dma_start(gfin[:, :], A["norm_final_2"].partition_broadcast(P)).then_inc(s_gfin, 16)

        @block.scalar
        def _(act):
            A_ = nc.scalar.activation
            chain = [0]

            def link(ins):
                chain[0] += 1
                ins.then_inc(s_act, 1)
                act.wait_ge(s_act, chain[0])

            def split_hi(us, i=0, n=UNIT):
                act.wait_ge(s_raw[us % NRAW], 16 * (us // NRAW + 1) + 16 * i)
                if not (isinstance(i, int) and us + 4 * i < 2):
                    act.wait_ge(s_mm, 4 * i + us - 1)
                A_(ring(w_hi, 2, us)[:, 0:n], ring(raw, NRAW, us)[:, 0:n], ACT.Copy).then_inc(s_hi, 1)

            def split_job(name, n):
                for j in range(n):
                    split_hi(U0[name] + j)

            def norm_sums(n, src, sem_, val):
                act.wait_ge(sem_, val)
                for T in range(2):
                    ins = A_(tok(xn, D, T), tok(src, D, T), ACT.Square, accum_out=ssq[:, T:T + 1])
                ins.then_inc(s_ssq, 1)
                act.wait_ge(s_var, n + 1)
                A_(std, var, ACT.Sqrt).then_inc(s_std, 1)

            def transposed_hi(k, dsts):
                for r in range(4):
                    act.wait_ge(s_tp, 4 * k + r + 1)
                    for j in range(2):
                        for g, hi in dsts:
                            c = 2 * r + j
                            src = bank(4 + r, S * j, S * j + S)
                            if g is None:
                                ins = A_(ch(hi, c), src, ACT.Copy)
                            else:
                                ins = A_(ch(hi, c), src, ACT.Copy, scale=gam[:, g + c:g + c + 1])
                    ins.then_inc(s_nhi, 1)

            def softmax_units(stage, units, psum_logits, table_free=None):
                a0, n = A0[stage], len(units)
                for i in range(n + 3):
                    if i < n:
                        a = a0 + i
                        act.wait_ge(s_m, a + 1)
                        w = units[i]["w"]
                        if psum_logits and a >= 2:
                            act.wait_ge(s_pt, a - 1)
                        for T in range(2):
                            dst = pb[:, 512 * (a % 2) + w[T][0]:512 * (a % 2) + w[T][1]]
                            src = bank(L0 + a % 2, *w[T]) if psum_logits else dst
                            ins = A_(dst, src, ACT.Exp, bias=nmax[a % 2][:, T:T + 1],
                                     accum_out=rsum[a % 2][:, T:T + 1])
                        ins.then_inc(s_e, 1)
                    if 1 <= i <= n:
                        a = a0 + i - 1
                        act.wait_ge(s_pt, a + 1)
                        if a >= 2:
                            act.wait_ge(s_pv, a - 1)
                        wd = units[i - 1]["w"][1][1]
                        A_(pt[:, 512 * (a % 2):512 * (a % 2) + wd], bank(TB + a % 2, 0, wd), ACT.Copy).then_inc(s_ptc, 1)
                    if i >= 3 and units[i - 3]["end"] is not None:
                        pair_hi(units[i - 3]["end"], s_pv, a0 + i - 2)

            def pair_hi(end, sem_, val):
                o, c = end
                act.wait_ge(sem_, val)
                A_(ch(m_hi, c), bank(OB + o % 2, 0, S), ACT.Copy).then_inc(s_ohi, 1)

            for dst, src in ((ident[:, :], A["ident"]), (gamrow[0:NGROW, :], A["gamma_rows"]),
                             (relb[0:32, :], A["rel_bias_2"]), (onehot[0:33, :], A["onehot"])):
                act.dma_start(dst, src).then_inc(s_cst, 16)
            act.dma_start(poolM[:, :], A["pool"]).then_inc(s_pin, 16)
            act.dma_start(wgrp[0:96, :].rearrange("p (c n) -> p c n", c=8),
                          A["a_w_group"].rearrange("g (c p) n -> p (g c) n", p=96)).then_inc(s_pin, 16)
            act.dma_start(sbc[:, :], A["sb_consts"]).then_inc(s_pin, 16)
            act.wait_ge(s_gamT, 1)
            A_(gam[:, 0:NGROW], bank(4, 0, NGROW), ACT.Copy).then_inc(s_gam, 1)
            act.wait_ge(s_tabp, 1)
            A_(stage[0:16, 0:512], ps[0:16, 5, 0:512], ACT.Copy).then_inc(s_tab, 1)
            act.wait_ge(s_gam, 1)

            def presplit(name):
                for j in range(2):
                    split_hi(U0[name] + j)

            def rest(name, n):
                for j in range(2, n):
                    split_hi(U0[name] + j)

            def empty_group(g, view, func=ACT.Copy, hi=512):
                A_(view, pair_banks(g % 2, 0, hi), func).then_inc(s_gact, 1)

            def both(t, cols, lo, n=512):
                return t[:, 0:2 * cols].rearrange("p (t n) -> p t n", t=2)[:, :, lo:lo + n]

            presplit("mem_a")
            norm_sums(0, memx, s_mem, 16)
            transposed_hi(0, [(0, m_hi)])
            norm_sums(1, x_sb, s_x, 16)
            transposed_hi(1, [(8, a_hi)])
            presplit("mem_b")
            act.wait_ge(s_mm, U0["mem_a"] + 2)
            empty_group(G0["mem_a"], both(kvm[:, 0:1024], 512, 0))
            presplit("in")
            act.wait_ge(s_mm, U0["mem_b"] + 2)
            empty_group(G0["mem_b"], both(kvm[:, 1024:2048], 512, 0))
            rest("in", 4)

            def empty_wide(name, dst, units):
                act.wait_ge(s_mm, U0[name] + units)
                for nb in range(2):
                    empty_group(G0[name] + nb, both(dst, D, 512 * nb))
            empty_wide("in", projA, 4)
            presplit("a_out")
            for r in range(4):
                act.wait_ge(s_pool, r + 1)
                A_(poolT[0:96, 512 * r:512 * r + 512], ps[0:96, 4 + r, :], ACT.Copy).then_inc(s_poolc, 1)
            for c in range(6):
                act.wait_ge(s_grp, c + 1)
                g = 8 * len(GAMMAS) + c
                A_(ch(m_hi, c), bank(c % 4, 0, S), ACT.Copy, scale=gam[:, g:g + 1]).then_inc(s_ghi, 1)

            def q_copy(k, dst, b, scale):
                act.wait_ge(s_qk, k + 1)
                A_(dst, bank(b), ACT.Copy, scale=scale).then_inc(s_qkc, 1)
            q_copy(0, qTA[:, :], 4, HD ** -0.5)
            q_copy(1, mkTA[:, :], 5, 1.0)
            softmax_units("mem_a", MEM_UNITS["mem_a"], True)
            rest("a_out", 4)

            def gated_act(name, done):
                def body(bs, i, last=False):
                    b_of = bs + 2 * i
                    if not last:
                        for q in range(2):
                            split_hi(U0[name] + 2 * bs + 2 + q, i)
                        act.wait_ge(s_mm, U0[name] + 2 * bs + 2 + 4 * i)
                        if not isinstance(b_of, int) or b_of >= 2:
                            act.wait_ge(s_gdve, emptied(G0[name] - 1, "dve") + b_of - 1)
                        g = mlp_a[:, 1024 * (bs % 2):1024 * (bs % 2) + 512].rearrange("p (t n) -> p t n", t=2)
                        A_(g, pair_banks((G0[name] + bs) % 2, 0, 256), ACT.Sigmoid).then_inc(s_sg, 1)
                    if last or not isinstance(b_of, int) or b_of >= 1:
                        b = bs - 1
                        act.wait_ge(s_ht, done + b + 1 + 2 * i)
                        A_(h_hi[:, bass.ds(512 * b + 1024 * i, 512)], bank(4 + b % 2), ACT.Copy).then_inc(s_hhi, 1)
                body(0, 0)
                with act.Fori(0, 5) as i:
                    body(1, i)
                    body(2, i)
                body(11, 0, last=True)

            presplit("a_gu")
            norm_sums(2, x_sb, s_gdve, emptied(G0["a_out"] + 1, "dve"))
            transposed_hi(2, [(16, a_hi)])
            act.wait_ge(s_tabd, 16)
            gated_act("a_gu", 0)
            rest("a_down", 11)

            presplit("kv")
            norm_sums(3, x_sb, s_gdve, emptied(G0["a_down"] + 1, "dve"))
            transposed_hi(3, [(24, a_hi), (32, m_hi)])
            for b in range(3):
                for q in range(2):
                    split_hi(U0["kv"] + 2 * b + 2 + q)
                act.wait_ge(s_mm, U0["kv"] + 2 * b + 2)
                empty_group(G0["kv"] + b, both(kvB, 2 * SB, 512 * b))
            rest("q", 4)
            empty_wide("q", qB, 4)
            presplit("b_out")
            for r, (t, c) in enumerate(B_ROUNDS):
                q_copy(2 + r, ch({"q": qTB, "k": kTB, "m": mkTB}[t], c, 2), 4 + r % 4, HD ** -0.5 if t == "q" else 1.0)
            for i in range(NSB + 3):
                if i < NSB:
                    act.wait_ge(s_z, i + 1)
                    e = sbE[:, 384 * (i % 2):384 * (i % 2) + 384]
                    if i >= 2:
                        act.wait_ge(s_sbl, i - 1)
                    link(A_(e, bank(L0 + i % 2, 0, 384), ACT.Abs))
                    link(A_(e, e, ACT.Exp, scale=-1.0))
                    A_(e, e, ACT.Ln, bias=1.0).then_inc(s_sbe, 1)
                if 1 <= i <= NSB:
                    act.wait_ge(s_arg, i)
                    w = sbW[:, 384 * ((i - 1) % 2):384 * ((i - 1) % 2) + 384]
                    A_(w, w, ACT.Exp).then_inc(s_wt, 1)
                if i >= 3 and (i - 3) % 2:
                    pair_hi((O0["sb"] + (i - 3) // 2, (i - 3) // 2), s_sbpv, i - 2)
            softmax_units("mem_b", MEM_UNITS["mem_b"], True)
            rest("b_out", 4)
            presplit("b_gu")
            norm_sums(4, x_sb, s_gdve, emptied(G0["b_out"] + 1, "dve"))
            transposed_hi(4, [(40, a_hi)])
            gated_act("b_gu", 11)
            rest("b_down", 11)

            presplit("front")
            norm_sums(5, x_sb, s_gdve, emptied(G0["b_down"] + 1, "dve"))
            norm_sums(6, x_sb, s_fin, 1)
            transposed_hi(5, [(48, a_hi)])
            for b in range(5):
                us = U0["front"] + 2 * b + 2
                if b < 3:
                    split_hi(us)
                    split_hi(us + 1)
                elif b == 3:
                    split_hi(us, n=8 * 192)
                    split_hi(us + 1)
                else:
                    split_hi(U0["cmp"] + 1)
                act.wait_ge(s_mm, min(us, U0["cmp"]))
                n = 512 if b < 4 else 192
                empty_group(G0["front"] + b, both(front, W_FRONT, 512 * b, n), hi=n)
            act.wait_ge(s_gact, emptied(G0["front_rest"], "act"))
            A_(gb.rearrange("p (t n) -> p t n", t=2), both(front, W_FRONT, C_GB, 24), ACT.Sigmoid).then_inc(s_gb, 1)
            act.wait_ge(s_peT, 1)
            A_(peT, bank(6, 0, 32), ACT.Copy).then_inc(s_pec, 1)
            act.wait_ge(s_x2p, 1)
            A_(x2h, pb[:, 0:960], ACT.Copy).then_inc(s_x2h, 1)
            for r in range(8):
                q_copy(10 + r, ch(TT, 2 * r, 2), 4 + (r + 3) % 4, HD ** -0.5 if r < 4 else 1.0)
            presplit("gates")
            act.wait_ge(s_uarg, 1)
            A_(gth, ga2, ACT.Tanh).then_inc(s_tanh, 1)
            act.wait_ge(s_cmpp, 1)
            A_(kcmpT, bank(6, 0, 30), ACT.Copy)
            A_(vcmp, bank(7, 0, 128), ACT.Copy).then_inc(s_cmpc, 1)
            act.wait_ge(s_clm, 1)
            A_(pc_v, pc_v, ACT.Exp).then_inc(s_cex, 1)
            act.wait_ge(s_cpt, 1)
            A_(pct[:, :], bank(5), ACT.Copy).then_inc(s_cptc, 1)
            for b in range(4):
                for q in range(2):
                    split_hi(U0["gates"] + 2 * b + 2 + q)
                act.wait_ge(s_mm, U0["gates"] + 2 * b + 2)
                empty_group(G0["gates"] + b, both(gates, 2 * D, 512 * b), ACT.Sigmoid)
            for h in range(8):
                act.wait_ge(s_ix, h + 1)
                if h >= 2:
                    act.wait_ge(s_ac, h - 1)
                A_(pt[:, 512 * (h % 2):512 * (h % 2) + 512], bank(L0 + h % 2), ACT.Relu).then_inc(s_rl, 1)
            softmax_units("nsa", NSA_UNITS, False)
            softmax_units("dsa", DSA_UNITS, False)
            presplit("branch_b")
            presplit("out2")
            transposed_hi(6, [(None, a_hi)])
            rest("out2", 4)
            presplit("up2")
            norm_sums(7, x_sb, s_gdve, emptied(G0["out2"] + 1, "dve"))
            transposed_hi(7, [(56, a_hi)])

            def up2(bs, i, last=False):
                b_of = bs + 2 * i
                if not last:
                    for q in range(2):
                        split_hi(U0["up2"] + 2 * bs + 2 + q, i)
                    act.wait_ge(s_mm, U0["up2"] + 2 * bs + 2 + 4 * i)
                    if not isinstance(b_of, int) or b_of >= 2:
                        act.wait_ge(s_hb, b_of - 1)
                    r = both(mlp_a[:, 1024 * (bs % 2):1024 * (bs % 2) + 1024], 512, 0)
                    A_(r, pair_banks((G0["up2"] + bs) % 2), ACT.Relu).then_inc(s_gact, 1)
                if last or not isinstance(b_of, int) or b_of >= 1:
                    b = bs - 1
                    act.wait_ge(s_ht, 22 + b + 1 + 2 * i)
                    A_(h_hi[:, bass.ds(1024 * b + 2048 * i, 1024)],
                       ps[:, 4 + 2 * (b % 2):6 + 2 * (b % 2), :].rearrange("p z n -> p (z n)"), ACT.Copy)\
                        .then_inc(s_hhi, 1)
            up2(0, 0)
            up2(1, 0)
            with act.Fori(0, 3) as i:
                up2(2, i)
                up2(3, i)
            up2(8, 0, last=True)
            rest("down2", 16)
            norm_sums(8, x_sb, s_gdve, emptied(G0["down2"] + 1, "dve"))

        @block.vector
        def _(dve):
            V = nc.vector
            chain = [0]

            def link(ins):
                chain[0] += 1
                ins.then_inc(s_dve, 1)
                dve.wait_ge(s_dve, chain[0])

            def split_lo(us, i=0, n=UNIT):
                dve.wait_ge(s_hi, us + 1 + 4 * i)
                V.tensor_tensor(ring(w_lo, 2, us)[:, 0:n], ring(raw, NRAW, us)[:, 0:n],
                                ring(w_hi, 2, us)[:, 0:n].bitcast(fp32), ALU.subtract).then_inc(s_lo, 1)

            def presplit(name):
                for j in range(2):
                    split_lo(U0[name] + j)

            def rest(name, n):
                for j in range(2, n):
                    split_lo(U0[name] + j)

            def norm_rows(n, src):
                dve.wait_ge(s_ssq, n + 1)
                V.tensor_scalar(var, ssq, 1.0 / D, EPS, ALU.mult, ALU.add).then_inc(s_var, 1)
                dve.wait_ge(s_std, n + 1)
                link(V.reciprocal(rst, std))
                link(V.tensor_tensor(t1, rst, rst, ALU.mult))
                link(V.tensor_tensor(t1, t1, var, ALU.mult))
                link(V.tensor_scalar(t1, t1, -0.5, 1.5, ALU.mult, ALU.add))
                link(V.tensor_tensor(rst, rst, t1, ALU.mult))
                for T in range(2):
                    ins = V.tensor_scalar(tok(xn, D, T), tok(src, D, T), rst[:, T:T + 1], None, ALU.mult)
                    ins.then_inc(s_xn, 1)

            def transposed_lo(k, dsts):
                for r in range(4):
                    dve.wait_ge(s_nhi, 4 * k + r + 1)
                    for j in range(2):
                        for g, hi, lo in dsts:
                            c = 2 * r + j
                            src, h = bank(4 + r, S * j, S * j + S), ch(hi, c).bitcast(fp32)
                            if g is None:
                                ins = V.tensor_tensor(ch(lo, c), src, h, ALU.subtract)
                            else:
                                ins = V.scalar_tensor_tensor(ch(lo, c), src, gam[:, g + c:g + c + 1], h,
                                                             ALU.mult, ALU.subtract)
                    ins.then_inc(s_nlo, 1)

            def add_to_x(name, units):
                dve.wait_ge(s_mm, U0[name] + units)
                for nb in range(2):
                    v = x_sb[:, :].rearrange("p (t n) -> p t n", t=2)[:, :, 512 * nb:512 * nb + 512]
                    V.tensor_tensor(v, v, pair_banks((G0[name] + nb) % 2), ALU.add).then_inc(s_gdve, 1)

            def pair_lo(end):
                o, c = end
                dve.wait_ge(s_ohi, o + 1)
                V.tensor_tensor(ch(m_lo, c), bank(OB + o % 2, 0, S), ch(m_hi, c).bitcast(fp32),
                                ALU.subtract).then_inc(s_olo, 1)

            def softmax_units(stage, units):
                a0, n = A0[stage], len(units)
                for i in range(n + 3):
                    if i < n:
                        a, u = a0 + i, units[i]
                        dve.wait_ge(s_lg, a + 1)
                        if u["bias"] is None:
                            V.tensor_reduce(nmax[a % 2], bank(L0 + a % 2).rearrange("p (t n) -> p t n", t=2),
                                            AX.X, ALU.max, negate=True).then_inc(s_m, 1)
                        else:
                            dve.wait_ge(s_pt, a - 1)
                            rows = [pb[:, 512 * (a % 2) + lo:512 * (a % 2) + hi] for lo, hi in u["w"]]
                            for T, (lo, hi) in enumerate(u["w"]):
                                b0 = 384 * u["bias"] + TABLE_J0 + 128 * T
                                add = V.tensor_tensor(rows[T], bank(L0 + a % 2, lo, hi),
                                                      strip[:, b0:b0 - (hi - lo):-1], ALU.add)
                            link(add)
                            if u["sel"]:
                                for T in range(2):
                                    n_ = 128 + 128 * T
                                    add = V.tensor_tensor(rows[T], rows[T], sel[:, 256 * T:256 * T + n_], ALU.add)
                                link(add)
                            for T in range(2):
                                ins = V.tensor_reduce(nmax[a % 2][:, T:T + 1], rows[T], AX.X, ALU.max, negate=True)
                            ins.then_inc(s_m, 1)
                    if 1 <= i <= n:
                        a, u = a0 + i - 1, units[i - 1]
                        dve.wait_ge(s_e, a + 1)
                        r = rrec[a % 2]
                        link(V.reciprocal(r, rsum[a % 2]))
                        if u["gate"] is not None:
                            g = gb.rearrange("p (t n) -> p t n", t=2)[:, :, u["gate"]]
                            link(V.tensor_tensor(r, r, g, ALU.mult))
                        for T, (lo, hi) in enumerate(u["w"]):
                            v = pb[:, 512 * (a % 2) + lo:512 * (a % 2) + hi]
                            ins = V.tensor_scalar(v, v, r[:, T:T + 1], None, ALU.mult)
                        ins.then_inc(s_p, 1)
                    if i >= 3 and units[i - 3]["end"] is not None:
                        pair_lo(units[i - 3]["end"])

            V.memset(relb[32:33, :], NEG).then_inc(s_dve, 1)
            V.memset(cw[:, 60:80], 0.0).then_inc(s_dve, 1)
            chain[0] += 2
            link(V.memset(pc[:, :], 0.0))

            presplit("mem_a")
            norm_rows(0, memx)
            transposed_lo(0, [(0, m_hi, m_lo)])
            norm_rows(1, x_sb)
            transposed_lo(1, [(8, a_hi, a_lo)])
            presplit("mem_b")
            presplit("in")
            rest("in", 4)
            presplit("a_out")
            for c in range(6):
                dve.wait_ge(s_ghi, c + 1)
                g = 8 * len(GAMMAS) + c
                V.scalar_tensor_tensor(ch(m_lo, c), bank(c % 4, 0, S), gam[:, g:g + 1], ch(m_hi, c).bitcast(fp32),
                                       ALU.mult, ALU.subtract).then_inc(s_glo, 1)
            softmax_units("mem_a", MEM_UNITS["mem_a"])
            rest("a_out", 4)

            def gated_dve(name, done):
                def body(bs, i, last=False):
                    b_of = bs + 2 * i
                    if not last:
                        for q in range(2):
                            split_lo(U0[name] + 2 * bs + 2 + q, i)
                        dve.wait_ge(s_sg, done + b_of + 1)
                        q = (G0[name] + bs) % 2
                        g = mlp_a[:, 1024 * (bs % 2):1024 * (bs % 2) + 512].rearrange("p (t n) -> p t n", t=2)
                        h = mlp_b[:, 1024 * (bs % 2):1024 * (bs % 2) + 512].rearrange("p (t n) -> p t n", t=2)
                        V.tensor_tensor(g, g, pair_banks(q, 0, 256), ALU.mult).then_inc(s_gm, 1)
                        dve.wait_ge(s_gm, done + b_of + 1)
                        if not isinstance(b_of, int) or b_of >= 2:
                            dve.wait_ge(s_ht, done + b_of - 1)
                        V.tensor_tensor(h, g, pair_banks(q, 256, 512), ALU.mult).then_inc(s_gdve, 1)
                    if last or not isinstance(b_of, int) or b_of >= 1:
                        b = bs - 1
                        dve.wait_ge(s_hhi, done + b + 1 + 2 * i)
                        cols = bass.ds(512 * b + 1024 * i, 512)
                        V.tensor_tensor(h_lo[:, cols], bank(4 + b % 2), h_hi[:, cols].bitcast(fp32), ALU.subtract)\
                            .then_inc(s_hlo, 1)
                body(0, 0)
                with dve.Fori(0, 5) as i:
                    body(1, i)
                    body(2, i)
                body(11, 0, last=True)

            add_to_x("a_out", 4)
            presplit("a_gu")
            norm_rows(2, x_sb)
            transposed_lo(2, [(16, a_hi, a_lo)])
            dve.wait_ge(s_tabd, 16)
            gated_dve("a_gu", 0)
            rest("a_down", 11)
            add_to_x("a_down", 11)

            presplit("kv")
            norm_rows(3, x_sb)
            transposed_lo(3, [(24, a_hi, a_lo), (32, m_hi, m_lo)])
            rest("kv", 6)
            presplit("q")
            rest("q", 4)
            presplit("b_out")
            dve.wait_ge(s_pin, 48)
            for i in range(NSB + 3):
                if i < NSB:
                    dve.wait_ge(s_sbe, i + 1)
                    if i >= 2:
                        dve.wait_ge(s_tri, i - 1)
                    e, l = (t[:, 384 * (i % 2):384 * (i % 2) + 384] for t in (sbE, sbL))
                    link(V.scalar_tensor_tensor(l, bank(L0 + i % 2, 0, 384), 0.0, e, ALU.max, ALU.add))
                    V.tensor_tensor(l, l, sb_mask, ALU.mult).then_inc(s_sbl, 1)
                if 1 <= i <= NSB:
                    h = i - 1
                    dve.wait_ge(s_tri, h + 1)
                    if h >= 2:
                        dve.wait_ge(s_sbpv, h - 1)
                    w = sbW[:, 384 * (h % 2):384 * (h % 2) + 384]
                    V.scalar_tensor_tensor(w, bank(L0 + h % 2, 0, 384), 0.0, sb_neg, ALU.min, ALU.add)\
                        .then_inc(s_arg, 1)
                if i >= 3 and (i - 3) % 2:
                    pair_lo((O0["sb"] + (i - 3) // 2, (i - 3) // 2))
            softmax_units("mem_b", MEM_UNITS["mem_b"])
            rest("b_out", 4)
            add_to_x("b_out", 4)
            presplit("b_gu")
            norm_rows(4, x_sb)
            transposed_lo(4, [(40, a_hi, a_lo)])
            gated_dve("b_gu", 11)
            rest("b_down", 11)
            add_to_x("b_down", 11)

            def final_rows(n, dst, load_no):
                norm_rows(n, x_sb)
                dve.wait_ge(s_xn, 2 * n + 2)
                dve.wait_ge(s_gfin, 16 * load_no)
                for T in range(2):
                    ins = V.tensor_tensor(tok(dst, D, T), tok(xn, D, T), gfin[:, :], ALU.mult)
                    if load_no == 2 or T:
                        ins.then_inc(s_fin, 1)
            presplit("front")
            final_rows(5, x_sb, 1)
            norm_rows(6, x_sb)
            transposed_lo(5, [(48, a_hi, a_lo)])
            rest("front", 8)
            split_lo(U0["front_rest"], n=8 * 192)
            presplit("cmp")
            dve.wait_ge(s_pec, 1)
            for n in range(2):
                dve.wait_ge(s_x2t, n + 1)
                for par in range(2):
                    for g in range(2):
                        src = ps[64 * par:64 * par + 64, 4 + n, S * g + par:S * g + par + 1]
                        src = bass.AP(src.tensor, src.offset, [src.ap[0], [2, 16], [16, 15]])
                        pe_ = peT[64 * par:64 * par + 64, 16 * n:16 * n + 1]
                        pe_ = bass.AP(pe_.tensor, pe_.offset, [pe_.ap[0], [1, 16], [0, 15]])
                        dst = pb[64 * par:64 * par + 64, 480 * n:480 * n + 480]\
                            .rearrange("p (j g n) -> p j g n", j=16, g=2)[:, :, g, :]
                        ins = V.tensor_tensor(dst, src, pe_, ALU.add)
            ins.then_inc(s_x2p, 1)
            dve.wait_ge(s_x2h, 1)
            V.tensor_tensor(x2l, pb[:, 0:960], x2h.bitcast(fp32), ALU.subtract).then_inc(s_x2, 1)
            dve.wait_ge(s_mm, U0["cmp"] + 2)
            link(V.tensor_copy(ga1, bank(4, 0, 60)))
            link(V.tensor_tensor(ga2, ga1, ga1, ALU.mult))
            link(V.tensor_scalar(ga2, ga2, 0.044715, 1.0, ALU.mult, ALU.add))
            link(V.tensor_tensor(ga2, ga2, ga1, ALU.mult))
            V.tensor_scalar(ga2, ga2, float(np.sqrt(2.0 / np.pi)), None, ALU.mult).then_inc(s_uarg, 1)
            dve.wait_ge(s_tanh, 1)
            link(V.tensor_scalar(gth, gth, 0.5, 0.5, ALU.mult, ALU.add))
            V.tensor_tensor(gel, gth, ga1, ALU.mult).then_inc(s_gel, 1)
            presplit("gates")
            dve.wait_ge(s_strip, 32)
            dve.wait_ge(s_clg, 1)
            for T in range(2):
                for odd in range(2):
                    v = pc[:, 256 * T:256 * T + 256].rearrange("p (h z n) -> p h z n", h=4, z=2)[:, :, odd, 0:15]
                    at = (8 + odd) * 384 + 224 + 128 * T
                    b_ = strip[:, at:at + 1]
                    b_ = bass.AP(b_.tensor, b_.offset, [b_.ap[0], [768, 4], [-16, 15]])
                    src = bank(4 + odd, 60 * T, 60 * T + 60).rearrange("p (h n) -> p h n", h=4)
                    ins = V.tensor_tensor(v, src, b_, ALU.add)
            link(ins)

            def per_row(t):
                return bass.AP(t.tensor, t.offset, [t.ap[0], [1, 16], [0, 15]])
            link(V.tensor_reduce(cmx, pc_v, AX.X, ALU.max))
            link(V.tensor_scalar(cmx, cmx, -1.0e20, None, ALU.max))
            V.tensor_tensor(pc_v, pc_v, per_row(cmx), ALU.subtract).then_inc(s_clm, 1)
            dve.wait_ge(s_cex, 1)
            link(V.tensor_reduce(csum, pc_v, AX.X, ALU.add))
            link(V.tensor_scalar(csum, csum, 1.0e-30, None, ALU.max))
            link(V.reciprocal(crec, csum))
            dve.wait_ge(s_gb, 1)
            link(V.tensor_tensor(crec.rearrange("p (t n) -> p t n", t=2), crec.rearrange("p (t n) -> p t n", t=2),
                                 gb.rearrange("p (t n) -> p t n", t=2)[:, :, 0:8], ALU.mult))
            V.tensor_tensor(pc_v, pc_v, per_row(crec), ALU.mult).then_inc(s_cp, 1)
            rest("gates", 8)
            presplit("branch_a")
            link(V.tensor_scalar(wi.rearrange("p (t n) -> p t n", t=2),
                                 front[:, :].rearrange("p (t n) -> p t n", t=2)[:, :, C_WI:C_WI + 8],
                                 (8 * 32) ** -0.5, None, ALU.mult))
            for h in range(8):
                dve.wait_ge(s_rl, h + 1)
                if h:
                    dve.wait_ge(s_ac, h)
                for T in range(2):
                    r = pt[:, 512 * (h % 2) + 256 * T:512 * (h % 2) + 256 * T + 256]
                    s_ = sc[:, 256 * T:256 * T + 256]
                    w = wi[:, 8 * T + h:8 * T + h + 1]
                    if h == 0:
                        ins = V.tensor_scalar(s_, r, w, None, ALU.mult)
                    else:
                        ins = V.scalar_tensor_tensor(s_, r, w, s_, ALU.mult, ALU.add)
                ins.then_inc(s_ac, 1)
            dve.wait_ge(s_ac, 8)
            link(V.tensor_tensor(sc[:, :], sc[:, :], caus[:, :], ALU.add))
            for rnd in range(S // 4 // 8):
                for T in range(2):
                    last = V.max(top8[:, 8 * T:8 * T + 8], sc[:, 256 * T:256 * T + 256])
                link(last)
                for T in range(2):
                    s_ = sc[:, 256 * T:256 * T + 256]
                    last = V.match_replace(s_, top8[:, 8 * T:8 * T + 8], s_, TAKEN)
                link(last)
            link(V.tensor_scalar(sel[:, :], sc[:, :], TAKEN, NEG, ALU.not_equal, ALU.mult))
            softmax_units("nsa", NSA_UNITS)
            softmax_units("dsa", DSA_UNITS)
            for n, name in enumerate(("branch_a", "branch_b")):
                presplit(("branch_b", "out2")[n])
                dve.wait_ge(s_mm, U0[name] + 2)
                for nb in range(2):
                    v = gates[:, :].rearrange("p (t n) -> p t n", t=2)[:, :, D * n + 512 * nb:D * n + 512 * nb + 512]
                    V.tensor_tensor(v, v, pair_banks((G0[name] + nb) % 2), ALU.mult).then_inc(s_gdve, 1)
            dve.wait_ge(s_gdve, emptied(G0["branch_b"] + 1, "dve"))
            gv = gates[:, :].rearrange("p (t n) -> p t n", t=2)
            V.tensor_tensor(gv[:, :, 0:D], gv[:, :, 0:D], gv[:, :, D:2 * D], ALU.add).then_inc(s_mx, 1)
            transposed_lo(6, [(None, a_hi, a_lo)])
            rest("out2", 4)
            add_to_x("out2", 4)
            presplit("up2")
            norm_rows(7, x_sb)
            transposed_lo(7, [(56, a_hi, a_lo)])

            def up2(bs, i, last=False):
                b_of = bs + 2 * i
                if not last:
                    for q in range(2):
                        split_lo(U0["up2"] + 2 * bs + 2 + q, i)
                    dve.wait_ge(s_gact, emptied(G0["up2"] - 1, "act") + b_of + 1)
                    if not isinstance(b_of, int) or b_of >= 2:
                        dve.wait_ge(s_ht, 22 + b_of - 1)
                    r = mlp_a[:, 1024 * (bs % 2):1024 * (bs % 2) + 1024]
                    V.tensor_tensor(mlp_b[:, 1024 * (bs % 2):1024 * (bs % 2) + 1024], r, r, ALU.mult)\
                        .then_inc(s_hb, 1)
                if last or not isinstance(b_of, int) or b_of >= 1:
                    b = bs - 1
                    dve.wait_ge(s_hhi, 22 + b + 1 + 2 * i)
                    cols = bass.ds(1024 * b + 2048 * i, 1024)
                    V.tensor_tensor(h_lo[:, cols], ps[:, 4 + 2 * (b % 2):6 + 2 * (b % 2), :].rearrange("p z n -> p (z n)"),
                                    h_hi[:, cols].bitcast(fp32), ALU.subtract).then_inc(s_hlo, 1)
            up2(0, 0)
            up2(1, 0)
            with dve.Fori(0, 3) as i:
                up2(2, i)
                up2(3, i)
            up2(8, 0, last=True)
            rest("down2", 16)
            add_to_x("down2", 16)
            final_rows(8, xn, 2)

        @block.tensor
        def _(pe):
            MM = nc.tensor.matmul

            def group_free(g):
                if g >= 2:
                    e = EMPTIED_BY[g - 2]
                    pe.wait_ge(s_gact if e == "act" else s_gdve, emptied(g - 2, e))

            def mult_unit(us, i, pieces, first, last, n=UNIT):
                pe.wait_ge(s_lo, us + 1 + 4 * i)
                wp = [ring(t, 2, us) for t in (w_hi, w_lo)]
                for kk, (c, act_parts, b, wd, off) in enumerate(pieces):
                    for pn, (ap_, wp_) in enumerate(PASSES):
                        for T in range(2):
                            ins = MM(ps[:, b + T, 0:wd], chT(act_parts[ap_], c, T), wp[wp_][:, off:off + wd],
                                     start=(c in first and pn == 0), stop=(c in last and pn == 2))
                ins.then_inc(s_mm, 1)

            def block_unit(us, i, q, b, parts, wd=512, nk=4):
                mult_unit(us, i, [(nk * q + k, parts, b, wd, wd * k) for k in range(nk)], (0,), (KC - 1,))

            def wide_job(name, n, parts, c0=0, ready=None):
                g = G0[name]
                group_free(g)
                group_free(g + 1)
                for j in range(n):
                    if ready:
                        ready(j)
                    mult_unit(U0[name] + j, 0, [(c0 + 2 * j + k, parts, 2 * ((g + nb) % 2), 512, D * k + 512 * nb)
                                                for nb in range(2) for k in range(2)], (c0,), (c0 + 2 * n - 1,))

            def block_job(name, n, parts, ready=None):
                for b in range(n):
                    group_free(G0[name] + b)
                    for q in range(2):
                        if b == 0 and ready:
                            ready(2 * q + 1)
                        block_unit(U0[name] + 2 * b + q, 0, q, 2 * ((G0[name] + b) % 2), parts)

            def normed(k):
                return lambda r: pe.wait_ge(s_nlo, 4 * k + r + 1)

            def transposes(k, src, sem_, vals):
                for r in range(4):
                    for j in range(2):
                        c = 2 * r + j
                        for T in range(2):
                            if r == 0 and j == 0:
                                pe.wait_ge(sem_, vals[T])
                            ins = nc.tensor.transpose(bank(4 + r, S * j + P * T, S * j + P * T + P),
                                                      src(T)[:, P * c:P * c + P], ident[:, :])
                    ins.then_inc(s_tp, 1)

            def norm_transposes(k, n):
                transposes(k, lambda T: tok(xn, D, T), s_xn, (2 * n + 1, 2 * n + 2))

            def softmax_units(stage, units, logits, values, free):
                a0, n = A0[stage], len(units)
                for i in range(n + 2):
                    if i < n:
                        a = a0 + i
                        if free and (i >= 2 or stage == "dsa"):
                            pe.wait_ge(free, a - 1)
                        logits(i, units[i], L0 + a % 2).then_inc(s_lg, 1)
                    if 1 <= i <= n:
                        a, u = a0 + i - 1, units[i - 1]
                        pe.wait_ge(s_p, a + 1)
                        if a >= 2:
                            pe.wait_ge(s_ptc, a - 1)
                        src = pb[:, 512 * (a % 2):512 * (a % 2) + 512]
                        for lo, to in u["tr"]:
                            ins = nc.tensor.transpose(bank(TB + a % 2, to, to + P), src[:, lo:lo + P], ident[:, :])
                        ins.then_inc(s_pt, 1)
                    if i >= 2:
                        a, u = a0 + i - 2, units[i - 2]
                        pe.wait_ge(s_ptc, a + 1)
                        if u["pair"][1] and u["pair"][0] >= 2:
                            pe.wait_ge(s_olo, u["pair"][0] - 1)
                        values(i - 2, u, pt[:, 512 * (a % 2):512 * (a % 2) + 512], OB + u["pair"][0] % 2)\
                            .then_inc(s_pv, 1)

            pe.wait_ge(s_cst, 64)
            nc.tensor.transpose(bank(4, 0, NGROW), gamrow[0:NGROW, :], ident[0:NGROW, 0:NGROW]).then_inc(s_gamT, 1)
            pe.wait_ge(s_dve, 3)
            MM(ps[0:16, 5, 0:512], relb[0:33, :], onehot[0:33, :], start=True, stop=True).then_inc(s_tabp, 1)
            pe.wait_ge(s_gam, 1)
            pe.wait_ge(s_tab, 1)
            MH, AH, HH = (m_hi, m_lo), (a_hi, a_lo), (h_hi, h_lo)
            norm_transposes(0, 0)
            normed(0)(3)
            norm_transposes(1, 1)
            block_job("mem_a", 1, MH)
            block_job("mem_b", 1, MH)
            wide_job("in", 4, AH, ready=normed(1))
            pe.wait_ge(s_pin, 48)
            pe.wait_ge(s_gact, emptied(G0["in"] + 1, "act"))
            for r in range(4):
                for c in (2 * r, 2 * r + 1):
                    o = S * (c % 2)
                    for T in range(2):
                        m0 = 1024 * T + S * (c // 2)
                        ins = MM(ps[0:96, 4 + r, o + P * T:o + S], tok(projA, D, T)[:, 96 * c:96 * c + 96],
                                 poolM[:, m0 + P * T:m0 + S], start=(T == 0), stop=(T == 1))
                ins.then_inc(s_pool, 1)
            for c in range(6):
                if c == 0:
                    pe.wait_ge(s_poolc, 4)
                if c >= 4:
                    pe.wait_ge(s_glo, c - 3)
                at = P * c
                while at < P * c + P:
                    g = at // 192
                    n = min(P * c + P, 192 * g + 192) - at
                    for cc in range(2):
                        k = 2 * g + cc
                        p0 = at - P * c
                        ins = MM(ps[p0:p0 + n, c % 4, 0:S], wgrp[0:96, 192 * k + at - 192 * g:192 * k + at - 192 * g + n],
                                 poolT[0:96, S * k:S * k + S], start=(cc == 0), stop=(cc == 1))
                    at += n
                ins.then_inc(s_grp, 1)

            def two_chunks(b, src):
                for c in range(2):
                    for T in range(2):
                        ins = nc.tensor.transpose(bank(b, S * c + P * T, S * c + P * T + P), src(c, T), ident[:, :])
                ins.then_inc(s_qk, 1)

            def mem_keys(l):
                return lambda c, T: kvm[:, 1024 * l + 512 * T + P * c:1024 * l + 512 * T + P * c + P]
            two_chunks(4, lambda c, T: tok(projA, D, T)[:, SB + P * c:SB + P * c + P])
            two_chunks(5, mem_keys(0))

            def mem_attention(stage, l, qT, mkT):
                def logits(h, u, b):
                    r = slice(64 * (h % 2), 64 * (h % 2) + 64)
                    for T in range(2):
                        ins = MM(bank(b, S * T, S * T + S), qT[r, S * (h // 2) + P * T:S * (h // 2) + P * T + P],
                                 mkT[r, S * (h // 2):S * (h // 2) + S], start=True, stop=True)
                    return ins

                def values(h, u, p_, o):
                    for M in range(2):
                        v0 = 1024 * l + 512 * M + 256 + HD * h
                        ins = MM(ps[64 * (h % 2):64 * (h % 2) + 64, o, 0:S], kvm[:, v0:v0 + HD],
                                 p_[:, S * M:S * M + S], start=(M == 0), stop=(M == 1))
                    return ins
                softmax_units(stage, MEM_UNITS[stage], logits, values, s_e)

            pe.wait_ge(s_qkc, 2)
            pe.wait_ge(s_glo, 6)
            mem_attention("mem_a", 0, qTA, mkTA)
            pe.wait_ge(s_olo, 2)
            wide_job("a_out", 4, MH)

            def gated_pe(name, done, k):
                def mult(bs, i):
                    b_of = bs + 2 * i
                    if isinstance(b_of, int):
                        group_free(G0[name] + bs)
                    else:
                        pe.wait_ge(s_gdve, emptied(G0[name] - 1, "dve") + b_of - 1)
                    for q in range(2):
                        if isinstance(b_of, int):
                            normed(k)(2 * q + 1)
                        block_unit(U0[name] + 2 * bs + q, i, q, 2 * ((G0[name] + bs) % 2), AH)

                def flip(bs, i, bound=False):
                    b_of = bs + 2 * i
                    pe.wait_ge(s_gdve, emptied(G0[name] - 1, "dve") + b_of + 1)
                    if not isinstance(b_of, int) or b_of >= 2 or done:
                        if not (isinstance(b_of, int) and done + b_of < 2):
                            pe.wait_ge(s_hlo, done + b_of - 1)
                    h = mlp_b[:, 1024 * (bs % 2):1024 * (bs % 2) + 512]
                    for c in range(2):
                        for T in range(2):
                            ins = nc.tensor.transpose(bank(4 + bs % 2, S * c + P * T, S * c + P * T + P),
                                                      h[:, 256 * T + P * c:256 * T + P * c + P], ident[:, :])
                    ins.then_inc(s_ht, 1)
                mult(0, 0)
                mult(1, 0)
                flip(0, 0)
                with pe.Fori(0, 4) as i:
                    mult(2, i)
                    flip(1, i)
                    mult(3, i)
                    flip(2, i)
                mult(10, 0)
                flip(9, 0)
                flip(10, 0)

            norm_transposes(2, 2)
            gated_pe("a_gu", 0, 2)
            wide_job("a_down", 11, HH, ready=lambda j: pe.wait_ge(s_hlo, j + 1))
            norm_transposes(3, 3)
            block_job("kv", 3, AH, ready=normed(3))
            wide_job("q", 4, MH)
            pe.wait_ge(s_gact, emptied(G0["q"] + 1, "act"))
            srcs = {"q": lambda c, T: tok(qB, D, T)[:, P * c:P * c + P],
                    "k": lambda c, T: tok(kvB, 2 * SB, T)[:, P * c:P * c + P], "m": mem_keys(1)}
            for r, (t, c0) in enumerate(B_ROUNDS):
                if r >= 4:
                    pe.wait_ge(s_qkc, 2 + r - 3)
                two_chunks(4 + r % 4, lambda c, T: srcs[t](c0 + c, T))
            pe.wait_ge(s_qkc, 10)
            pe.wait_ge(s_pin, 48)
            for i in range(NSB + 2):
                if i < NSB:
                    r, c = slice(64 * (i % 2), 64 * (i % 2) + 64), S * (i // 2)
                    if i >= 2:
                        pe.wait_ge(s_arg, i - 1)
                    b = L0 + i % 2
                    MM(bank(b, 0, 256), kTB[r, c:c + P], qTB[r, c:c + S], start=True, stop=False,
                       skip_group_check=True)
                    MM(bank(b, 256, 384), kTB[r, c + P:c + S], qTB[r, c + P:c + S], start=False, stop=False,
                       skip_group_check=True).then_inc(s_z, 1)
                if 1 <= i <= NSB:
                    h = i - 1
                    b = L0 + h % 2
                    pe.wait_ge(s_sbl, h + 1)
                    l = sbL[:, 384 * (h % 2):384 * (h % 2) + 384]
                    MM(bank(b, 0, 256), sb_tri, l[:, 0:256], start=False, stop=False, skip_group_check=True)
                    MM(bank(b, 128, 256), sb_ones, l[:, 256:384], start=False, stop=False, skip_group_check=True)
                    MM(bank(b, 256, 384), sb_tri, l[:, 256:384], start=False, stop=True, skip_group_check=True)\
                        .then_inc(s_tri, 1)
                if i >= 2:
                    h = i - 2
                    o = O0["sb"] + h // 2
                    pe.wait_ge(s_wt, h + 1)
                    if h % 2 == 0:
                        pe.wait_ge(s_olo, o - 1)
                    w = sbW[:, 384 * (h % 2):384 * (h % 2) + 384]
                    out = ps[64 * (h % 2):64 * (h % 2) + 64, OB + o % 2, 0:S]
                    MM(out, tok(kvB, 2 * SB, 0)[:, SB + HD * h:SB + HD * h + HD], w[:, 0:256], start=True, stop=False)
                    MM(out[:, P:S], tok(kvB, 2 * SB, 1)[:, SB + HD * h:SB + HD * h + HD], w[:, 256:384],
                       start=False, stop=True).then_inc(s_sbpv, 1)
            mem_attention("mem_b", 1, qTB[:, 6 * S:8 * S], mkTB)
            pe.wait_ge(s_olo, O0["nsa"])
            wide_job("b_out", 4, MH)
            norm_transposes(4, 4)
            gated_pe("b_gu", 11, 4)
            wide_job("b_down", 11, HH, ready=lambda j: pe.wait_ge(s_hlo, 11 + j + 1))

            norm_transposes(5, 6)
            block_job("front", 4, AH, ready=normed(5))
            group_free(G0["front_rest"])
            block_unit(U0["front_rest"], 0, 0, 2 * (G0["front_rest"] % 2), AH, wd=192, nk=8)
            pe.wait_ge(s_gact, emptied(G0["front_rest"], "act"))
            pe.wait_ge(s_ind, 64)

            def flip64(b, col, src_col, n=64, copies=2):
                for T in range(2):
                    for q in range(copies):
                        ins = MM(ps[n * q:n * q + n, b, col + P * T:col + P * T + P],
                                 tok(front, W_FRONT, T)[:, src_col:src_col + n], ident[:, :], start=True, stop=True)
                return ins
            nc.tensor.transpose(bank(6, 0, 32), per, ident[0:32, 0:32]).then_inc(s_peT, 1)
            for n in range(2):
                for g in range(2):
                    ins = flip64(4 + n, S * g, (C_KC, C_VC)[n] + HD * g)
                ins.then_inc(s_x2t, 1)
            for r in range(8):
                b = 4 + (r + 3) % 4
                if r == 1:
                    pe.wait_ge(s_x2p, 1)
                if r >= 4:
                    pe.wait_ge(s_qkc, 10 + r - 3)
                if r == 3:
                    pe.wait_ge(s_pec, 1)
                if r < 5:
                    c0 = (C_QA, C_QA + 256, C_QB, C_QB + 256, C_QI)[r]
                    two_chunks(b, lambda c, T: tok(front, W_FRONT, T)[:, c0 + P * c:c0 + P * c + P])
                elif r == 5:
                    flip64(b, 0, C_KA)
                    flip64(b, S, C_KI, n=32, copies=4).then_inc(s_qk, 1)
                else:
                    c0 = (C_KS, C_KW)[r - 6]
                    flip64(b, 0, c0)
                    flip64(b, S, c0 + HD).then_inc(s_qk, 1)
            pe.wait_ge(s_x2, 1)
            pe.wait_ge(s_qkc, 18)
            for n in range(2):
                us = U0["cmp"] + n
                pe.wait_ge(s_lo, us + 1)
                wp = [ring(t, 2, us) for t in (w_hi, w_lo)]
                for j in range(16):
                    for pn, (xp, wq) in enumerate(PASSES):
                        ins = MM(bank(4, 30 * n, 30 * n + 30), wp[wq][:, P * j:P * j + P],
                                 (x2h, x2l)[xp][:, 480 * n + 30 * j:480 * n + 30 * j + 30],
                                 start=(j == 0 and pn == 0), stop=(j == 15 and pn == 2))
                ins.then_inc(s_mm, 1)
            pe.wait_ge(s_gel, 1)
            for q in range(2):
                MM(ps[64 * q:64 * q + 64, 6, 0:30], w2[:, 0:HD], gel[:, 0:30], start=True, stop=True)
            for g in range(2):
                for q in range(4):
                    ins = MM(ps[32 * q:32 * q + 32, 7, HD * g:HD * g + HD], cw[:, 30 + 15 * g:62 + 15 * g],
                             w2[:, HD:2 * HD], start=True, stop=True)
            ins.then_inc(s_cmpp, 1)
            pe.wait_ge(s_cmpc, 1)

            def q_head(slot0, h, T):
                return TT[64 * (h % 2):64 * (h % 2) + 64, S * (slot0 + h // 2) + P * T:S * (slot0 + h // 2) + P * T + P]
            for T in range(2):
                for h in range(8):
                    c0 = 60 * T + 15 * (h // 2)
                    r = slice(64 * (h % 2), 64 * (h % 2) + 64)
                    ins = MM(bank(4 + h % 2, c0, c0 + 15), q_head(4, h, T), kcmpT[r, 15 * (h // 4):15 * (h // 4) + 15],
                             start=True, stop=True)
            ins.then_inc(s_clg, 1)
            pe.wait_ge(s_cp, 1)
            for hh in range(2):
                for T in range(2):
                    ins = nc.tensor.transpose(bank(5, S * hh + P * T, S * hh + P * T + P),
                                              pc[:, S * T + P * hh:S * T + P * hh + P], ident[:, :])
            ins.then_inc(s_cpt, 1)
            block_job("gates", 4, AH)
            pe.wait_ge(s_cptc, 1)
            for h in range(8):
                r = slice(32 * (h % 4), 32 * (h % 4) + 32)
                if h >= 2:
                    pe.wait_ge(s_rl, h - 1)
                for T in range(2):
                    c0 = S * (8 + h // 4) + P * T
                    ins = MM(bank(L0 + h % 2, S * T, S * T + S), TT[r, c0:c0 + P], TT[r, 11 * S:12 * S],
                             start=True, stop=True)
                ins.then_inc(s_ix, 1)

            def causal_attention(stage, units, q_slot):
                def logits(i, u, b):
                    h = u["head"]
                    k_ = TT[64 * (h % 2):64 * (h % 2) + 64, S * u["k"]:S * u["k"] + S]
                    MM(bank(b, 0, P), q_head(q_slot, h, 0), k_[:, 0:P], start=True, stop=True)
                    return MM(bank(b, P, P + S), q_head(q_slot, h, 1), k_, start=True, stop=True)

                def values(i, u, p_, o):
                    h = u["head"]
                    out = ps[64 * (h % 2):64 * (h % 2) + 64, o, 0:S]
                    if u["cmp"]:
                        q0 = 32 * (h % 4)
                        MM(out, vcmp[q0:q0 + 15, HD * (h // 4):HD * (h // 4) + HD],
                           pct[q0:q0 + 15, S * (h // 4):S * (h // 4) + S], start=True, stop=False)
                    v = [tok(front, W_FRONT, T)[:, u["v"]:u["v"] + HD] for T in range(2)]
                    MM(out, v[0], p_[:, 0:S], start=u["first"] and not u["cmp"], stop=False)
                    return MM(out[:, P:S], v[1], p_[:, S:S + P], start=False, stop=u["last"])
                softmax_units(stage, units, logits, values, s_m)
            pe.wait_ge(s_rl, 8)
            pe.wait_ge(s_gact, emptied(G0["gates"] + 3, "act"))
            causal_attention("nsa", NSA_UNITS, 4)
            causal_attention("dsa", DSA_UNITS, 0)
            pe.wait_ge(s_olo, O0["dsa"] + 4)
            wide_job("branch_a", 2, MH)
            wide_job("branch_b", 2, MH, c0=4)
            transposes(6, lambda T: tok(gates, 2 * D, T), s_mx, (1, 1))
            wide_job("out2", 4, AH, ready=normed(6))
            norm_transposes(7, 7)

            def up_mult(bs, i):
                b_of = bs + 2 * i
                if isinstance(b_of, int):
                    group_free(G0["up2"] + bs)
                else:
                    pe.wait_ge(s_gact, emptied(G0["up2"] - 1, "act") + b_of - 1)
                for q in range(2):
                    if isinstance(b_of, int):
                        normed(7)(2 * q + 1)
                    block_unit(U0["up2"] + 2 * bs + q, i, q, 2 * ((G0["up2"] + bs) % 2), AH)

            def up_flip(bs, i):
                b_of = bs + 2 * i
                pe.wait_ge(s_hb, b_of + 1)
                pe.wait_ge(s_hlo, 22 + b_of - 1)
                h = mlp_b[:, 1024 * (bs % 2):1024 * (bs % 2) + 1024]
                for c in range(4):
                    for T in range(2):
                        o = S * (c % 2) + P * T
                        ins = nc.tensor.transpose(bank(4 + 2 * (bs % 2) + c // 2, o, o + P),
                                                  h[:, 512 * T + P * c:512 * T + P * c + P], ident[:, :])
                ins.then_inc(s_ht, 1)
            up_mult(0, 0)
            up_mult(1, 0)
            up_flip(0, 0)
            with pe.Fori(0, 3) as i:
                up_mult(2, i)
                up_flip(1, i)
                up_mult(3, i)
                up_flip(2, i)
            up_flip(7, 0)
            wide_job("down2", 16, HH, ready=lambda j: pe.wait_ge(s_hlo, 22 + j // 2 + 1))


B_ROUNDS = [("k", 0), ("k", 2), ("k", 4), ("q", 0), ("q", 2), ("q", 4), ("q", 6), ("m", 0)]
NSB = SB // HD
WHOLE, CAUSAL = ((0, 256), (256, 512)), ((0, 128), (128, 384))


def units_of(o0, chunk0, heads):
    out = []
    for h, branches in enumerate(heads):
        for n, b in enumerate(branches):
            end = h % 2 == 1 and n == len(branches) - 1
            out.append({"bias": None, "sel": False, "gate": None, "cmp": False, "head": h, "first": n == 0,
                        "last": n == len(branches) - 1, "pair": (o0 + h // 2, h % 2 == 0 and n == 0),
                        "end": (o0 + h // 2, chunk0 + h // 2) if end else None, **b})
    return out


TR_WHOLE = [(256 * T + 128 * M, 256 * M + 128 * T) for M in range(2) for T in range(2)]
TR_CAUSAL = [(0, 0), (128, 128), (256, 256)]
MEM_UNITS = {s: units_of(O0[s], 6, [[{"w": WHOLE, "tr": TR_WHOLE}]] * 4) for s in ("mem_a", "mem_b")}
NSA_UNITS = units_of(O0["nsa"], 4, [[
    {"w": CAUSAL, "tr": TR_CAUSAL, "bias": 8 + h, "gate": 8 + h, "k": 12 + h // 4, "v": C_VS + HD * (h // 4),
     "cmp": True},
    {"w": CAUSAL, "tr": TR_CAUSAL, "bias": 8 + h, "gate": 16 + h, "k": 14 + h // 4, "v": C_VW + HD * (h // 4)}]
    for h in range(8)])
DSA_UNITS = units_of(O0["dsa"], 0, [[
    {"w": CAUSAL, "tr": TR_CAUSAL, "bias": h, "sel": True, "k": 10, "v": C_VA}] for h in range(8)])


def _constants():
    import math
    i = np.arange(P)
    le = (i[:, None] < i[None, :]).astype(np.float32)
    one = np.ones((P, P), np.float32)
    tri = -(i[:, None] >= i[None, :]).astype(np.float32)
    neg = np.where(le > 0, 0.0, NEG).astype(np.float32)
    sb = np.concatenate([tri, -one, le, one, le, neg, 0 * one, neg], axis=1)
    t = np.arange(S)
    pool = np.zeros((2, P, 4, S), np.float32)
    for g, w in enumerate((2, 4, 8, 16)):
        m = ((t[None, :] - t[:, None] >= 0) & (t[None, :] - t[:, None] < w)) / np.minimum(t + 1, w)[None, :]
        pool[:, :, g, :] = (m - np.eye(S)).reshape(2, P, S)
    causal = np.where(t[None, :] <= t[:, None], 0.0, NEG).astype(np.float32)
    dist = np.arange(512) - TABLE_J0
    n = np.maximum(dist, 0)
    nf = np.maximum(n, 1).astype(np.float32)
    large = 16 + (np.log(nf / np.float32(16)) / np.float32(math.log(128 / 16)) * np.float32(16)).astype(np.int32)
    bucket = np.where(n < 16, n, np.minimum(large, 31))
    onehot = np.zeros((33, 512), np.float32)
    onehot[np.where(dist < 0, 32, bucket), np.arange(512)] = 1.0
    return {"ident": np.eye(P, dtype=np.float32), "sb_consts": np.ascontiguousarray(sb, np.float32),
            "pool": np.ascontiguousarray(pool.transpose(1, 0, 2, 3).reshape(P, 2 * 4 * S)),
            "causal": np.ascontiguousarray(causal.reshape(2, P, S).transpose(1, 0, 2).reshape(P, 2 * S)),
            "onehot": onehot}


def kernel(**inputs):
    import concourse.bacc as _bacc
    from concourse.bass_utils import run_bass_kernel_spmd as _run

    nc = _bacc.Bacc("TRN2", target_bir_lowering=False, num_devices=1)
    arrays, A = {}, {}

    def give(name, a):
        a = np.ascontiguousarray(a)
        arrays[f"in_{name}"] = a
        A[name] = nc.dram_tensor(f"in_{name}", a.shape, mybir.dt.from_np(a.dtype), kind="ExternalInput").ap()

    raw = {n: np.asarray(a) for n, a in inputs.items()}

    def wide(w):
        return w.reshape(-1, 2, P, D).transpose(0, 2, 1, 3).reshape(-1, UNIT)

    def blocks(w):
        return w.reshape(2, 4, P, -1, 512).transpose(3, 0, 2, 1, 4).reshape(-1, UNIT)

    def gated(w):
        return w.reshape(2, 4, P, 2, -1, 256).transpose(4, 0, 2, 1, 3, 5).reshape(-1, UNIT)

    w_in_2 = raw["w_in_2"][0]
    for name, w in (("mem_a", blocks(raw["a_w_mem_kv"][0])), ("mem_b", blocks(raw["b_w_mem_kv"][0])),
                    ("in", wide(raw["a_w_in"][0])), ("a_out", wide(raw["a_w_out"][0])),
                    ("a_gu", gated(raw["a_w_gu"][0])), ("a_down", wide(raw["a_w_down"][0])),
                    ("kv", blocks(raw["w_kv"])), ("q", wide(raw["b_w_q"][0])), ("b_out", wide(raw["b_w_out"][0])),
                    ("b_gu", gated(raw["b_w_gu"][0])), ("b_down", wide(raw["b_w_down"][0])),
                    ("front", blocks(w_in_2[:, 0:2048])),
                    ("front_rest", w_in_2[:, 2048:W_FRONT].reshape(KC, P, 192).transpose(1, 0, 2).reshape(P, -1)),
                    ("cmp", np.concatenate([raw[f"cmp_w1_{k}_2"][0].reshape(16, P, P).transpose(1, 0, 2)
                                            .reshape(P, UNIT) for k in "kv"], axis=0)),
                    ("gates", blocks(w_in_2[:, W_FRONT:])), ("branch_a", wide(raw["w_branch_a_2"][0])),
                    ("branch_b", wide(raw["w_branch_b_2"][0])), ("out2", wide(raw["w_out_2"][0])),
                    ("up2", blocks(raw["w_mlp_in_2"][0])), ("down2", wide(raw["w_mlp_out_2"][0]))):
        give(name, w)
    for n in ("x", "mem", "a_w_group", "cmp_pe_k_2", "cmp_w2_k_2", "cmp_pe_v_2", "cmp_w2_v_2"):
        give(n, raw[n][0])
    for n in ("final_norm", "norm_final_2", "rel_bias_2"):
        give(n, raw[n])
    give("gamma_rows", np.concatenate([raw[n].reshape(-1, P) for n in GAMMAS + ["a_scale"]], axis=0))
    for n, a in _constants().items():
        give(n, a)
    A["table"] = nc.dram_tensor("distance_table", (16, 512), mybir.dt.float32).ap()
    A["out"] = nc.dram_tensor("out_0", (S, D), mybir.dt.float32, kind="ExternalOutput").ap()
    build(nc, A)
    r = _run(nc, [arrays], core_ids=[0])
    return r.results[0]["out_0"].reshape(1, S, D)
```
